# Optimizing a Trainium2 kernel written in Bass

```python
import math
import jax, jax.numpy as jnp
from jax import lax
import numpy as np

D_MODEL = 1024
BATCH = 1
SEQ = 512
DEPTH = 1
DEC_BATCH = 1
DEC_SEQ = 2048
PAST_LEN = 128

MIX_WIDTH = D_MODEL
FOURIER_WIDTH = D_MODEL // 2
N_FOURIER_GROUPS = 4
FOURIER_GROUP = FOURIER_WIDTH // N_FOURIER_GROUPS
HEAD_DIM = 64
N_HEADS = (MIX_WIDTH - FOURIER_WIDTH) // HEAD_DIM
N_KV_HEADS = 2
Q_PER_KV = N_HEADS // N_KV_HEADS
ATTN_WIDTH = N_HEADS * HEAD_DIM
KV_WIDTH = N_KV_HEADS * HEAD_DIM
IN_WIDTH = FOURIER_WIDTH + ATTN_WIDTH + 2 * KV_WIDTH
WINDOW = 128
BLOCK = 128
D_FF = 4 * D_MODEL
LN_EPS = 1e-5
DEEPNORM_ALPHA = (2.0 * DEPTH) ** 0.25
DEEPNORM_BETA = (8.0 * DEPTH) ** -0.25
NEG_BIG = -1e30

kernel_name = 'hymba_fnet_swa_alibi_deepnorm_encoder'

def layer_norm(x, g, b):
    xf = x.astype(jnp.float32)
    mu = jnp.mean(xf, axis=-1, keepdims=True)
    var = jnp.mean(jnp.square(xf - mu), axis=-1, keepdims=True)
    y = (xf - mu) * lax.rsqrt(var + LN_EPS) * g.astype(jnp.float32) + b.astype(jnp.float32)
    return y.astype(x.dtype)

def alibi_slopes():
    h = jnp.arange(N_HEADS, dtype=jnp.float32)
    return jnp.exp2(-8.0 * (h + 1.0) / N_HEADS)

def fourier_mix(u, w_fourier):
    B, S, _ = u.shape
    ug = u.reshape(B, S, N_FOURIER_GROUPS, FOURIER_GROUP).astype(jnp.float32)
    f = jnp.real(jnp.fft.fft2(ug, axes=(1, 3), norm='ortho')).astype(u.dtype)
    out = jnp.einsum('bsgc,gcd->bsgd', f, w_fourier)
    return out.reshape(B, S, FOURIER_WIDTH)

def windowed_attention(q, k, v, sink_logits):
    B, S, _ = q.shape
    nb = S // BLOCK
    qb = q.reshape(B, nb, BLOCK, N_KV_HEADS, Q_PER_KV, HEAD_DIM)

    def band(t):
        t = t.reshape(B, S, N_KV_HEADS, HEAD_DIM)
        tp = jnp.pad(t, ((0, 0), (WINDOW, WINDOW), (0, 0), (0, 0)))
        tp = tp.reshape(B, nb + 2, BLOCK, N_KV_HEADS, HEAD_DIM)
        return jnp.concatenate([tp[:, :-2], tp[:, 1:-1], tp[:, 2:]], axis=2)

    kb = band(k)
    vb = band(v)
    scale = 1.0 / math.sqrt(HEAD_DIM)
    scores = jnp.einsum('bnqkgd,bnskd->bnkgqs', qb, kb,
                        preferred_element_type=jnp.float32) * scale

    qi = jnp.arange(BLOCK)
    si = jnp.arange(3 * BLOCK)
    rel = si[None, :] - WINDOW - qi[:, None]
    dist = jnp.abs(rel).astype(jnp.float32)
    key_pos = jnp.arange(nb)[:, None] * BLOCK + si[None, :] - WINDOW
    valid = (jnp.abs(rel) <= WINDOW)[None, :, :] & ((key_pos >= 0) & (key_pos < S))[:, None, :]

    slopes = alibi_slopes().reshape(N_KV_HEADS, Q_PER_KV)
    scores = scores - slopes[:, :, None, None] * dist
    scores = jnp.where(valid[None, :, None, None], scores, NEG_BIG)

    sink = sink_logits.astype(jnp.float32).reshape(N_KV_HEADS, Q_PER_KV)[None, None, :, :, None, None]
    m = jnp.maximum(jnp.max(scores, axis=-1, keepdims=True), sink)
    p = jnp.exp(scores - m)
    denom = jnp.sum(p, axis=-1, keepdims=True) + jnp.exp(sink - m)
    probs = (p / denom).astype(v.dtype)
    out = jnp.einsum('bnkgqs,bnskd->bnqkgd', probs, vb)
    return out.reshape(B, S, ATTN_WIDTH)

def encoder_layer(x, w_in, w_fourier, sink_logits, w_out, ln_mix_g, ln_mix_b,
                  w_ff1, w_ff2, ln_ffn_g, ln_ffn_b):
    proj = x @ w_in
    c1 = FOURIER_WIDTH
    c2 = c1 + ATTN_WIDTH
    c3 = c2 + KV_WIDTH
    u = proj[..., :c1]
    q = proj[..., c1:c2]
    k = proj[..., c2:c3]
    v = proj[..., c3:]
    heads = jnp.concatenate([fourier_mix(u, w_fourier),
                             windowed_attention(q, k, v, sink_logits)], axis=-1)
    x = layer_norm(DEEPNORM_ALPHA * x + heads @ w_out, ln_mix_g, ln_mix_b)
    h = jnp.square(jax.nn.relu(x @ w_ff1))
    x = layer_norm(DEEPNORM_ALPHA * x + h @ w_ff2, ln_ffn_g, ln_ffn_b)
    return x

def trunk(x, ln_emb_g, ln_emb_b, w_in, w_fourier, sink_logits, w_out, ln_mix_g, ln_mix_b,
          w_ff1, w_ff2, ln_ffn_g, ln_ffn_b):
    x = layer_norm(x, ln_emb_g, ln_emb_b)
    for l in range(DEPTH):
        x = encoder_layer(x, w_in[l], w_fourier[l], sink_logits[l], w_out[l],
                          ln_mix_g[l], ln_mix_b[l], w_ff1[l], w_ff2[l],
                          ln_ffn_g[l], ln_ffn_b[l])
    return x

def setup_inputs(seed: int = 0) -> dict:
    key = jax.random.key(seed)
    ks = jax.random.split(key, 16)
    f32 = jnp.float32
    nrm = lambda k, shape, s: jax.random.normal(k, shape, f32) * s
    return {
        'x_prompt': nrm(ks[0], (BATCH, SEQ, D_MODEL), 1.0),
        'x_sample': nrm(ks[1], (DEC_BATCH, DEC_SEQ, D_MODEL), 1.0),
        'ln_emb_g': 1.0 + nrm(ks[2], (D_MODEL,), 0.02),
        'ln_emb_b': nrm(ks[3], (D_MODEL,), 0.02),
        'w_in': nrm(ks[4], (DEPTH, D_MODEL, IN_WIDTH), D_MODEL ** -0.5),
        'w_fourier': nrm(ks[5], (DEPTH, N_FOURIER_GROUPS, FOURIER_GROUP, FOURIER_GROUP), FOURIER_GROUP ** -0.5),
        'sink_logits': nrm(ks[6], (DEPTH, N_HEADS), 0.5),
        'w_out': nrm(ks[7], (DEPTH, MIX_WIDTH, D_MODEL), DEEPNORM_BETA * MIX_WIDTH ** -0.5),
        'ln_mix_g': 1.0 + nrm(ks[8], (DEPTH, D_MODEL), 0.02),
        'ln_mix_b': nrm(ks[9], (DEPTH, D_MODEL), 0.02),
        'w_ff1': nrm(ks[10], (DEPTH, D_MODEL, D_FF), D_MODEL ** -0.5),
        'w_ff2': nrm(ks[11], (DEPTH, D_FF, D_MODEL), DEEPNORM_BETA * D_FF ** -0.5),
        'ln_ffn_g': 1.0 + nrm(ks[12], (DEPTH, D_MODEL), 0.02),
        'ln_ffn_b': nrm(ks[13], (DEPTH, D_MODEL), 0.02),
    }

def reference(x_prompt, x_sample, ln_emb_g, ln_emb_b, w_in, w_fourier, sink_logits, w_out,
              ln_mix_g, ln_mix_b, w_ff1, w_ff2, ln_ffn_g, ln_ffn_b):
    y_prompt = trunk(x_prompt, ln_emb_g, ln_emb_b, w_in, w_fourier, sink_logits, w_out,
                     ln_mix_g, ln_mix_b, w_ff1, w_ff2, ln_ffn_g, ln_ffn_b)
    y_sample = trunk(x_sample, ln_emb_g, ln_emb_b, w_in, w_fourier, sink_logits, w_out,
                     ln_mix_g, ln_mix_b, w_ff1, w_ff2, ln_ffn_g, ln_ffn_b)
    return (y_prompt, y_sample)


_drawn_inputs = setup_inputs


def setup_inputs(seed=0):
    import zlib

    import numpy as np

    out = dict(_drawn_inputs(seed))
    spreads = {}
    factors = {'ln_emb_b': 2.796,
     'sink_logits': 8.0,
     'ln_mix_g': 7.653,
     'ln_mix_b': 7.287,
     'ln_ffn_g': 8.284,
     'ln_ffn_b': 7.924}
    for name, (base, spread) in spreads.items():
        noise = np.random.default_rng([zlib.crc32(name.encode()), seed]).standard_normal(out[name].shape)
        drawn = base * np.exp(spread * noise) if base else spread * noise
        out[name] = __import__('jax').numpy.asarray(drawn.astype(out[name].dtype))
    for name, factor in factors.items():
        out[name] = (out[name] * factor).astype(out[name].dtype)
    return out
```

```python
import math
from contextlib import ExitStack

import numpy as np

import concourse.bass as bass
from concourse import mybir

F32 = mybir.dt.float32
F32R = mybir.dt.float32r
ACT = mybir.ActivationFunctionType
ALU = mybir.AluOpType

P = 128
D = 1024
KT = D // P
SEQS = ((0, 512), (512, 2048))
TOK = sum(s for _, s in SEQS)
GRP = 512
NG = TOK // GRP
TPG = GRP // P
NT = TOK // P
FOUR = 512
NFG = 4
HD = 64
NH = 8
NKV = 2
QPK = NH // NKV
IN_W = FOUR + NH * HD + 2 * NKV * HD
KROW = FOUR + NH * HD
FT = KROW // P + 1
FF = 4 * D
EPS = 1e-5
ALPHA = 2.0 ** 0.25
QSCALE = -1.0 / math.sqrt(HD)
BIG = 1e30


def slices(seq_len):
    half = seq_len // 2
    chunks = -(-(half + 1) // 512)
    width = -(-(half + 1) // chunks)
    width += width % 2
    return half // P + 1, half // P, width, chunks


def split_mm(tensor, out, w_hi, w_lo, m_hi, m_lo, first, last):
    tensor.matmul(out, w_lo, m_hi, start=first, stop=False)
    tensor.matmul(out, w_hi, m_lo, start=False, stop=False)
    return tensor.matmul(out, w_hi, m_hi, start=False, stop=last)


class Phase:

    def __init__(self, nc, ctx, phase):
        self.nc, self.ctx, self.phase, self.used = nc, ctx, phase, []
        ctx.callback(self.release)

    def release(self):
        if self.used:
            self.nc.clear_and_free_semaphores(self.used)
            self.nc.all_engine_barrier()

    def sb(self, name, shape, dt=F32):
        return self.ctx.enter_context(self.nc.sbuf_tensor(f"{self.phase}_{name}", shape, dt))

    def ps(self, name, shape):
        return self.ctx.enter_context(self.nc.psum_tensor(f"{self.phase}_{name}", shape, F32))

    def sem(self, name):
        self.used.append(self.nc.alloc_semaphore(f"{self.phase}_{name}"))
        return self.used[-1]

    def sems(self, name, n):
        return [self.sem(f"{name}{i}") for i in range(n)]


def embed_project(nc, x, ln_g, ln_b, w_in, ident_d, xn_d, proj_d, v_d):
    with ExitStack() as ctx:
        al = Phase(nc, ctx, "a")
        ident = al.sb("ident", [P, P])
        gain = al.sb("gain", [P, D])
        shift = al.sb("shift", [P, D])
        w_raw = al.sb("w_raw", [P, 2, IN_W])
        w_hi = al.sb("w_hi", [P, KT, IN_W], F32R)
        w_lo = al.sb("w_lo", [P, KT, IN_W], F32R)
        x_in = al.sb("x_in", [P, TPG, D])
        x_nrm = al.sb("x_nrm", [P, TPG, D])
        xg = al.sb("xg", [P, 2, D])
        stats = al.sb("stats", [P, TPG, 2, 6])
        mv = al.sb("mv", [P, TPG, 2])
        var_eps = al.sb("var_eps", [P, TPG])
        rstd = al.sb("rstd", [P, TPG])
        mhalf = al.sb("mhalf", [P, TPG])
        eps = al.sb("eps", [P, TPG])
        xt_hi = al.sb("xt_hi", [P, KT, GRP], F32R)
        xt_lo = al.sb("xt_lo", [P, KT, GRP], F32R)
        stage = al.sb("stage", [P, 5, GRP])
        bank = al.ps("bank", [P, 8, 512])

        const_in, mhalf_set = al.sem("const_in"), al.sem("mhalf_set")
        w_in_ld, w_hi_done, w_split = al.sems("w_in_ld", 2), al.sem("w_hi_done"), al.sem("w_split")
        x_ld, x_free = al.sems("x_ld", TPG), al.sem("x_free")
        stats_done, var_done, rstd_done = al.sem("stats_done"), al.sem("var_done"), al.sem("rstd_done")
        xn_ready = al.sem("xn_ready")
        xn_st = al.sems("xn_st", TPG)
        turned, xt_hi_done, xt_done = al.sem("turned"), al.sem("xt_hi_done"), al.sem("xt_done")
        proj_done, stage_done = al.sem("proj_done"), al.sem("stage_done")
        stage_st = al.sems("stage_st", 5)
        UNITS = FT + 1

        block = ctx.enter_context(nc.Block())

        @block.sync
        def _(sp):
            sp.dma_start(ident[:], ident_d).then_inc(const_in, 16)
            sp.dma_start(gain[:], ln_g.partition_broadcast(P)).then_inc(const_in, 16)
            sp.dma_start(shift[:], ln_b.partition_broadcast(P)).then_inc(const_in, 16)
            for k in range(KT):
                if k >= 2:
                    sp.wait_ge(w_split, k - 1)
                sp.dma_start(w_raw[:, k % 2, :], w_in[k * P:(k + 1) * P, :]).then_inc(w_in_ld[k % 2], 16)
            with sp.Fori(0, NG) as g:
                for j in range(TPG):
                    sp.wait_ge(xn_ready, g * TPG + j + 1)
                    sp.dma_start(xn_d[bass.ds(g * GRP + j * P, P), :], x_nrm[:, j, :]).then_inc(xn_st[j], 16)
                for m in (1, 0, *range(2, UNITS)):
                    if m:
                        sp.wait_ge(stage_done, g * UNITS + UNITS + m + 1)
                    if m < FT:
                        sp.dma_start(proj_d[m * P:(m + 1) * P, bass.ds(g * GRP, GRP)],
                                     stage[:, m % 5, :]).then_inc(stage_st[m % 5], 16)
                    else:
                        sp.dma_start(v_d[bass.ds(g * GRP, GRP), :].rearrange("(t p) c -> p t c", p=P),
                                     stage[:, m % 5, :].rearrange("p (t c) -> p t c", t=TPG)
                                     ).then_inc(stage_st[m % 5], 16)
            for j in range(TPG):
                sp.wait_ge(xn_st[j], 16 * (NG + 1))
            for s in range(5):
                sp.wait_ge(stage_st[s], 16 * (2 * NG + 1))

        @block.gpsimd
        def _(pool):
            def load_x(g, first):
                for j in range(TPG):
                    if not first:
                        pool.wait_ge(x_free, (g - 1) * TPG + j + 1)
                    pool.dma_start(x_in[:, j, :], x[bass.ds(g * GRP + j * P, P), :]).then_inc(x_ld[j], 16)

            def inverse_std(g):
                pool.wait_ge(stats_done, g * TPG + TPG)
                pool.tensor_tensor(var_eps[:], mv[:, :, 1], eps[:], ALU.add).then_inc(var_done, 1)
                pool.wait_ge(var_done, g + 1)
                pool.tensor_tensor(rstd[:], var_eps[:], mhalf[:], ALU.pow).then_inc(rstd_done, 1)

            load_x(0, True)
            pool.memset(mhalf[:], -0.5).then_inc(mhalf_set, 1)
            pool.memset(eps[:], EPS).then_inc(mhalf_set, 1)
            for k in range(KT):
                pool.wait_ge(w_hi_done, k + 1)
                pool.tensor_tensor(w_lo[:, k, :], w_raw[:, k % 2, :], w_hi[:, k, :].bitcast(F32),
                                   ALU.subtract).then_inc(w_split, 1)
            pool.wait_ge(mhalf_set, 2)
            with pool.Fori(0, NG - 1) as g:
                inverse_std(g)
                load_x(g + 1, False)
            inverse_std(NG - 1)

        @block.vector
        def _(dve):
            with dve.Fori(0, NG) as g:
                for j in range(TPG):
                    dve.wait_ge(x_ld[j], g * 16 + 16)
                    for h in range(2):
                        dve.bn_stats(stats[:, j, h, :], x_in[:, j, h * 512:(h + 1) * 512])
                dve.drain()
                for j in range(TPG):
                    dve.bn_aggr(mv[:, j, :], stats[:, j, :, :]).then_inc(stats_done, 1)
                dve.drain()
                dve.wait_ge(const_in, 48)
                dve.wait_ge(rstd_done, g + 1)
                for j in range(TPG):
                    dve.scalar_tensor_tensor(xg[:, j % 2, :], x_in[:, j, :], mv[:, j, 0:1], gain[:], ALU.subtract,
                                             ALU.mult).then_inc(x_free, 1)
                    dve.drain()
                    dve.wait_ge(turned, g * KT + KT)
                    dve.wait_ge(xn_st[j], g * 16 + 16)
                    dve.scalar_tensor_tensor(x_nrm[:, j, :], xg[:, j % 2, :], rstd[:, j:j + 1], shift[:], ALU.mult,
                                             ALU.add).then_inc(xn_ready, 1)
                for k in range(KT):
                    dve.wait_ge(xt_hi_done, g * KT + k + 1)
                    dve.tensor_tensor(xt_lo[:, k, :], bank[:, k, :], xt_hi[:, k, :].bitcast(F32),
                                      ALU.subtract).then_inc(xt_done, 1)

        @block.scalar
        def _(act):
            for s in range(5):
                act.sem_inc(stage_st[s], 16)
            for j in range(TPG):
                act.sem_inc(xn_st[j], 16)
            act.sem_inc(stage_done, UNITS)
            for k in range(KT):
                act.wait_ge(w_in_ld[k % 2], 16 * (k // 2 + 1))
                act.copy(w_hi[:, k, :], w_raw[:, k % 2, :]).then_inc(w_hi_done, 1)
            with act.Fori(0, NG) as g:
                for k in range(KT):
                    act.wait_ge(turned, g * KT + KT + k + 1)
                    act.copy(xt_hi[:, k, :], bank[:, k, :]).then_inc(xt_hi_done, 1)
                for m in range(UNITS):
                    act.wait_ge(proj_done, g * UNITS + m + 1)
                    act.wait_ge(stage_st[m % 5], g * 32 + (m // 5) * 16 + 16)
                    is_q = FOUR // P <= m < KROW // P
                    act.mul(stage[:, m % 5, :], bank[:, m % 8, :], QSCALE if is_q else 1.0
                            ).then_inc(stage_done, 1)

        @block.tensor
        def _(pe):
            pe.sem_inc(turned, KT)
            pe.wait_ge(const_in, 48)
            with pe.Fori(0, NG) as g:
                for k in range(KT):
                    if k == 0:
                        pe.wait_ge(xn_ready, g * TPG + TPG)
                    pe.wait_ge(stage_done, g * UNITS + (k + 9 if k < UNITS - 8 else k + 1))
                    for j in range(TPG):
                        mm = pe.transpose(bank[:, k, j * P:(j + 1) * P], x_nrm[:, j, k * P:(k + 1) * P],
                                          ident[:])
                    mm.then_inc(turned, 1)
                for m in range(UNITS):
                    out = bank[:, m % 8, :]
                    if m >= 8:
                        pe.wait_ge(stage_done, g * UNITS + UNITS + m - 7)
                    if m < FT:
                        cols = slice(m * P, (m + 1) * P)
                        for k in range(KT):
                            if m == 0:
                                pe.wait_ge(w_split, k + 1)
                                pe.wait_ge(xt_done, g * KT + k + 1)
                            mm = split_mm(pe, out, w_hi[:, k, cols], w_lo[:, k, cols], xt_hi[:, k, :],
                                          xt_lo[:, k, :], k == 0, k == KT - 1)
                    else:
                        cols = slice(m * P, (m + 1) * P)
                        for t in range(TPG):
                            tok = slice(t * P, (t + 1) * P)
                            for k in range(KT):
                                mm = split_mm(pe, out[:, tok], xt_hi[:, k, tok], xt_lo[:, k, tok],
                                              w_hi[:, k, cols], w_lo[:, k, cols], k == 0, k == KT - 1)
                    mm.then_inc(proj_done, 1)


def fourier(nc, name, tok0, seq_len, proj_d, w_fourier, chan_d, table_d, heads_d):
    NE, NO, W, CH = slices(seq_len)
    half = seq_len // 2
    EW, OW = NE * P, NO * P
    quads = [("e", a, min(a + 4, NE)) for a in range(0, NE, 4)] + [("o", a, min(a + 4, NO)) for a in range(0, NO, 4)]
    NQ = len(quads)
    with ExitStack() as outer:
        alo = Phase(nc, outer, name)
        z_hi = alo.sb("z_hi", [P, NE + NO, FOUR], F32R)
        z_lo = alo.sb("z_lo", [P, NE + NO, FOUR], F32R)
        bank = alo.ps("bank", [P, 8, 512])

        with ExitStack() as ctx:
            al = Phase(nc, ctx, name + "z")
            chan = al.sb("chan", [P, 2, P])
            wf = al.sb("wf", [P, NFG, P])
            ab_hi = al.sb("ab_hi", [P, 2, FOUR], F32R)
            ab_lo = al.sb("ab_lo", [P, 2, FOUR], F32R)
            u_raw = al.sb("u_raw", [P, 2, seq_len])
            fold = al.sb("fold", [P, EW + OW])
            f_hi = al.sb("f_hi", [P, 2, EW + OW], F32R)
            f_lo = al.sb("f_lo", [P, 2, EW + OW], F32R)

            in_ld, u_ld = al.sem("in_ld"), al.sems("u_ld", 2)
            ab_done, ab_hi_done, ab_split = al.sem("ab_done"), al.sem("ab_hi_done"), al.sem("ab_split")
            even_done, odd_done = al.sem("even_done"), al.sem("odd_done")
            f_hi_done, f_split = al.sem("f_hi_done"), al.sem("f_split")
            z_done, z_hi_done, z_split = al.sem("z_done"), al.sem("z_hi_done"), al.sem("z_split")
            block = ctx.enter_context(nc.Block())

            @block.sync
            def _(sp):
                sp.dma_start(chan[:], chan_d).then_inc(in_ld, 16)
                sp.dma_start(wf[:], w_fourier.rearrange("g c d -> c g d")).then_inc(in_ld, 16)
                for g in range(NFG):
                    if g >= 2:
                        sp.wait_ge(even_done, g - 1)
                        sp.wait_ge(odd_done, g - 1)
                    sp.dma_start(u_raw[:, g % 2, :], proj_d[g * P:(g + 1) * P, tok0:tok0 + seq_len]
                                 ).then_inc(u_ld[g % 2], 16)

            @block.gpsimd
            def _(pool):
                for g in range(NFG):
                    u = u_raw[:, g % 2, :]
                    pool.wait_ge(u_ld[g % 2], 16 * (g // 2 + 1))
                    if g:
                        pool.wait_ge(f_split, g)
                    pool.tensor_tensor(fold[:, EW:EW + 1], u[:, 0:1], u[:, 0:1], ALU.subtract)
                    pool.tensor_tensor(fold[:, EW + 1:EW + OW], u[:, 1:half],
                                       u[:, seq_len - 1:half:-1], ALU.subtract).then_inc(odd_done, 1)

            @block.vector
            def _(dve):
                for i in range(2):
                    dve.wait_ge(ab_hi_done, i + 1)
                    dve.tensor_tensor(ab_lo[:, i, :], bank[:, i, :], ab_hi[:, i, :].bitcast(F32),
                                      ALU.subtract).then_inc(ab_split, 1)

                def z_rest(g):
                    for q, (kind, a, b) in enumerate(quads):
                        base = a if kind == "e" else NE + a
                        out = slice(base, base + b - a)
                        cols = slice(g * P, (g + 1) * P)
                        dve.wait_ge(z_hi_done, g * NQ + q + 1)
                        dve.tensor_tensor(z_lo[:, out, cols],
                                          bank[:, 2 + q, 0:(b - a) * P].rearrange("p (s d) -> p s d", d=P),
                                          z_hi[:, out, cols].bitcast(F32), ALU.subtract).then_inc(z_split, 1)

                dve.memset(fold[:, half + 1:EW], 0.0)
                for g in range(NFG):
                    u = u_raw[:, g % 2, :]
                    dve.wait_ge(u_ld[g % 2], 16 * (g // 2 + 1))
                    if g:
                        dve.wait_ge(f_split, g)
                    dve.tensor_copy(fold[:, 0:1], u[:, 0:1])
                    dve.tensor_copy(fold[:, half:half + 1], u[:, half:half + 1])
                    dve.tensor_tensor(fold[:, 1:half], u[:, 1:half], u[:, seq_len - 1:half:-1], ALU.add)
                    dve.drain().then_inc(even_done, 1)
                    dve.wait_ge(f_hi_done, g + 1)
                    dve.tensor_tensor(f_lo[:, g % 2, :], fold[:], f_hi[:, g % 2, :].bitcast(F32), ALU.subtract
                                      ).then_inc(f_split, 1)
                    if g:
                        z_rest(g - 1)
                z_rest(NFG - 1)

            @block.scalar
            def _(act):
                for i in range(2):
                    act.wait_ge(ab_done, i + 1)
                    act.copy(ab_hi[:, i, :], bank[:, i, :]).then_inc(ab_hi_done, 1)

                def z_high(g):
                    for q, (kind, a, b) in enumerate(quads):
                        base = a if kind == "e" else NE + a
                        act.wait_ge(z_done, g * NQ + q + 1)
                        act.copy(z_hi[:, base:base + b - a, g * P:(g + 1) * P],
                                 bank[:, 2 + q, 0:(b - a) * P].rearrange("p (s d) -> p s d", d=P)
                                 ).then_inc(z_hi_done, 1)
                for g in range(NFG):
                    act.wait_ge(even_done, g + 1)
                    act.wait_ge(odd_done, g + 1)
                    if g >= 2:
                        act.wait_ge(z_done, NQ * (g - 1))
                    act.copy(f_hi[:, g % 2, :], fold[:]).then_inc(f_hi_done, 1)
                    if g:
                        z_high(g - 1)
                z_high(NFG - 1)

            @block.tensor
            def _(pe):
                pe.wait_ge(in_ld, 32)
                for i in range(2):
                    pe.matmul(bank[:, i, :], chan[:, i, :], wf[:].rearrange("p g d -> p (g d)"), start=True,
                              stop=True).then_inc(ab_done, 1)
                for g in range(NFG):
                    for q, (kind, a, b) in enumerate(quads):
                        if q == 0:
                            pe.wait_ge(f_split, g + 1)
                        if g == 0:
                            pe.wait_ge(ab_split, 2)
                        else:
                            pe.wait_ge(z_split, (g - 1) * NQ + q + 1)
                        i = int(kind == "o")
                        cols = slice(g * P, (g + 1) * P)
                        for s in range(a, b):
                            pos = slice((EW if i else 0) + s * P, (EW if i else 0) + (s + 1) * P)
                            mm = split_mm(pe, bank[:, 2 + q, (s - a) * P:(s - a + 1) * P],
                                          f_hi[:, g % 2, pos], f_lo[:, g % 2, pos], ab_hi[:, i, cols],
                                          ab_lo[:, i, cols], True, True)
                        mm.then_inc(z_done, 1)

        with ExitStack() as ctx:
            al = Phase(nc, ctx, name + "s")
            NT_ = NE + NO
            t_raw = al.sb("t_raw", [P, 4, W])
            slots = min(2, CH)
            t_hi = al.sb("t_hi", [P, slots, NT_, W], F32R)
            t_lo = al.sb("t_lo", [P, slots, NT_, W], F32R)
            odd = al.sb("odd", [P, 2, W])
            fwd = al.sb("fwd", [P, 2, W])
            rev = al.sb("rev", [P, 2, W])

            t_ld, t_hi_done, t_split = al.sems("t_ld", 4), al.sem("t_hi_done"), al.sem("t_split")
            even_done, odd_done, odd_read = al.sem("even_done"), al.sem("odd_done"), al.sem("odd_read")
            out_done, fwd_st, rev_st = al.sem("out_done"), al.sems("fwd_st", 2), al.sems("rev_st", 2)
            block = ctx.enter_context(nc.Block())

            @block.gpsimd
            def _(pool):
                for i in range(CH * NT_):
                    c, s = divmod(i, NT_)
                    if i >= 4:
                        pool.wait_ge(t_split, i - 3)
                    pool.dma_start(t_raw[:, i % 4, :], table_d[s * P:(s + 1) * P, c * W:(c + 1) * W]
                                   ).then_inc(t_ld[i % 4], 16)

            @block.scalar
            def _(act):
                def table(i):
                    c, s = divmod(i, NT_)
                    act.wait_ge(t_ld[i % 4], 16 * (i // 4 + 1))
                    if c >= slots:
                        act.wait_ge(even_done, NFG * (c - slots + 1))
                    act.copy(t_hi[:, c % slots, s, :], t_raw[:, i % 4, :]).then_inc(t_hi_done, 1)

                def copy_odd(n):
                    act.wait_ge(even_done, n + 1)
                    if n >= 2:
                        act.wait_ge(out_done, n - 1)
                    act.copy(odd[:, n % 2, :], bank[:, 2 * (n % 4) + 1, 0:W]).then_inc(odd_done, 1)
                ahead = list(range(CH * NT_))
                for i in range(min(slots * NT_, len(ahead))):
                    table(i)
                done = slots * NT_
                for n in range(CH * NFG):
                    copy_odd(n)
                    if n % NFG == NFG - 1:
                        while done < min((n // NFG + 1 + slots) * NT_, CH * NT_):
                            table(done)
                            done += 1

            @block.vector
            def _(dve):
                def rest(i):
                    c, s = divmod(i, NT_)
                    dve.wait_ge(t_hi_done, i + 1)
                    dve.tensor_tensor(t_lo[:, c % slots, s, :], t_raw[:, i % 4, :],
                                      t_hi[:, c % slots, s, :].bitcast(F32), ALU.subtract).then_inc(t_split, 1)

                def combine(n):
                    even = bank[:, 2 * (n % 4), 0:W]
                    dve.wait_ge(odd_done, n + 1)
                    if n >= 2:
                        dve.wait_ge(fwd_st[n % 2], 16 * (n // 2))
                        dve.wait_ge(rev_st[n % 2], 16 * (n // 2))
                    dve.tensor_tensor(fwd[:, n % 2, :], even, odd[:, n % 2, :], ALU.subtract)
                    dve.tensor_tensor(rev[:, n % 2, W - 1::-1], even, odd[:, n % 2, :], ALU.add)
                    dve.drain().then_inc(out_done, 1)
                done = min(slots, CH) * NT_
                for i in range(done):
                    rest(i)
                for n in range(CH * NFG):
                    combine(n)
                    if n % NFG == NFG - 1:
                        while done < min((n // NFG + 1 + slots) * NT_, CH * NT_):
                            rest(done)
                            done += 1

            @block.tensor
            def _(pe):
                for n in range(CH * NFG):
                    c, g = divmod(n, NFG)
                    cols = slice(g * P, (g + 1) * P)
                    if n >= 4:
                        pe.wait_ge(out_done, n - 3)
                    for s in range(NT_):
                        if g == 0:
                            pe.wait_ge(t_split, c * NT_ + s + 1)
                        which = int(s >= NE)
                        mm = split_mm(pe, bank[:, 2 * (n % 4) + which, 0:W], z_hi[:, s, cols], z_lo[:, s, cols],
                                      t_hi[:, c % slots, s, :], t_lo[:, c % slots, s, :], s in (0, NE),
                                      s in (NE - 1, NT_ - 1))
                    mm.then_inc(even_done, 1)

            @block.sync
            def _(sp):
                for n in range(CH * NFG):
                    c, g = divmod(n, NFG)
                    rows = slice(g * P, (g + 1) * P)
                    sp.wait_ge(out_done, n + 1)
                    sp.dma_start(heads_d[rows, tok0 + c * W:tok0 + (c + 1) * W], fwd[:, n % 2, :]
                                 ).then_inc(fwd_st[n % 2], 16)
                    sp.wait_ge(fwd_st[n % 2], 16 * (n // 2 + 1))
                    top = tok0 + seq_len - c * W + 1
                    sp.dma_start(heads_d[rows, top - W:top], rev[:, n % 2, :]).then_inc(rev_st[n % 2], 16)
                for s in range(2):
                    sp.wait_ge(rev_st[s], 16 * (CH * NFG // 2))


def attend(nc, proj_d, v_d, sink, bias_d, ident_d, heads_d):
    NB = NT
    with ExitStack() as ctx:
        al = Phase(nc, ctx, "c")
        ident = al.sb("ident", [P, P])
        bias = al.sb("bias", [P, NH, 3 * P])
        neg_sink = al.sb("neg_sink", [P, NH])
        snk = al.sb("snk", [P, NH])
        k_raw = al.sb("k_raw", [P, NKV, GRP])
        ka = al.sb("ka", [P, NKV, TOK], F32R)
        kb = al.sb("kb", [P, NKV, TOK], F32R)
        v_raw = al.sb("v_raw", [P, NB, NKV, HD])
        vv = al.sb("vv", [P, NB, NKV, 2, HD], F32R)
        q_raw = al.sb("q_raw", [P, 2, NH, P])
        qs = al.sb("qs", [P, 2, NH, P], F32R)
        prob = al.sb("prob", [P, 4, 3 * P])
        nmax = al.sb("nmax", [P, 2, NH])
        esink = al.sb("esink", [P, 2, NH])
        esum = al.sb("esum", [P, 2, NH])
        den = al.sb("den", [P, 2, NH])
        rden = al.sb("rden", [P, 2, NH])
        pt_hi = al.sb("pt_hi", [P, 2, 3 * P], F32R)
        pt_lo = al.sb("pt_lo", [P, 2, 3 * P], F32R)
        o_lo = al.sb("o_lo", [P, 2, NH, HD])
        o_sum = al.sb("o_sum", [P, 2, NH, HD])
        o_nrm = al.sb("o_nrm", [P, 2, NH, HD])
        ot = al.sb("ot", [P, 2, 4, P])
        sc = al.ps("sc", [P, 2, 512])
        pt = al.ps("pt", [P, 2, 512])
        pv = al.ps("pv", [P, 2, 4, P])
        tr = al.ps("tr", [P, 2, 4, P])

        const_in, sink_neg = al.sem("const_in"), al.sem("sink_neg")
        k_ld, k_rounded, k_split = al.sem("k_ld"), al.sem("k_rounded"), al.sem("k_split")
        v_ld, v_hi_done, v_split = al.sem("v_ld"), al.sem("v_hi_done"), al.sem("v_split")
        q_ld, q_rounded, q_split = al.sems("q_ld", 2), al.sem("q_rounded"), al.sem("q_split")
        sc_done, biased, exp_done = al.sem("sc_done"), al.sem("biased"), al.sem("exp_done")
        pt_done, pt_hi_done, pt_split = al.sem("pt_done"), al.sem("pt_hi_done"), al.sem("pt_split")
        pv_done, sink_arg, sink_exp = al.sem("pv_done"), al.sem("sink_arg"), al.sem("sink_exp")
        o_lo_done, o_sum_done, o_nrm_done = al.sem("o_lo_done"), al.sem("o_sum_done"), al.sem("o_nrm_done")
        tr_done, ot_done, ot_st = al.sem("tr_done"), al.sem("ot_done"), al.sems("ot_st", 2)
        block = ctx.enter_context(nc.Block())

        FIRST, MID, LAST = (1, 2), (0, 1, 2), (0, 1)
        firsts = [t // P for t, _ in SEQS]
        lasts = [(t + s) // P - 1 for t, s in SEQS]

        def window(b):
            return FIRST if b in firsts else LAST if b in lasts else MID

        def blocks(eng, body):
            b = 0
            while b < NB:
                run = 0
                while b and b + run + 1 < NB and window(b + run) == MID and window(b + run + 1) == MID:
                    run += 1
                if run >= 4:
                    pairs = run // 2
                    with eng.Fori(0, pairs) as i:
                        for j in range(2):
                            body(i * 2 + (b + j), (b + j) % 2, MID, MID)
                    b += 2 * pairs
                else:
                    body(b, b % 2, window(b), window(b + 1) if b + 1 < NB else None)
                    b += 1

        def wait(eng, sem, count):
            if not isinstance(count, int) or count > 0:
                eng.wait_ge(sem, count)

        def ahead(b, s, h, kbs, nxt):
            if h + 2 < NH:
                return b, s, h + 2, kbs
            return (b + 1, 1 - s, h + 2 - NH, nxt) if nxt else None

        passed, passed_pool, passed_dve = al.sem("passed"), al.sem("passed_pool"), al.sem("passed_dve")
        heads_v = heads_d[FOUR:, :].rearrange("(k p) t -> p k t", p=P)
        q_view = proj_d[FOUR:KROW, :].rearrange("(h d) t -> d h t", d=HD)

        @block.sync
        def _(sp):
            sp.dma_start(bias[:], bias_d).then_inc(const_in, 16)
            sp.dma_start(snk[:], sink.partition_broadcast(P)).then_inc(const_in, 16)
            sp.dma_start(ident[:], ident_d).then_inc(const_in, 16)
            for g in range(NG):
                if g:
                    sp.wait_ge(k_split, 2 * g)
                for half in range(2):
                    sp.dma_start(k_raw[half * HD:(half + 1) * HD, :, :],
                                 proj_d[KROW:KROW + P, g * GRP:(g + 1) * GRP].rearrange("(v d) t -> d v t", d=HD)
                                 ).then_inc(k_ld, 16)
                if g == 0:
                    sp.dma_start(v_raw[:], v_d.rearrange("(b p) (v d) -> p b v d", p=P, d=HD)).then_inc(v_ld, 16)

            def store(b, s, kbs, nxt):
                sp.wait_ge(ot_done, b + 1)
                sp.sem_inc(passed, 1)
                sp.dma_start(heads_v[:, :, bass.ds(b * P, P)], ot[:, s, :, :]).then_inc(ot_st[s], 16)
            blocks(sp, store)
            for s in range(2):
                sp.wait_ge(ot_st[s], 16 * (NB // 2))

        @block.gpsimd
        def _(pool):
            def load_q(b, s):
                wait(pool, q_split, b - 1)
                for half in range(2):
                    pool.dma_start(q_raw[half * HD:(half + 1) * HD, s, :, :], q_view[:, :, bass.ds(b * P, P)]
                                   ).then_inc(q_ld[s], 16)

            def round_q(b, s):
                wait(pool, sc_done, (b - 1) * NH)
                pool.sem_inc(passed_pool, 1)
                pool.wait_ge(q_ld[s], (b - s) * 16 + 32)
                pool.sem_inc(passed_pool, 1)
                pool.tensor_copy(qs[:, s, :, :], q_raw[:, s, :, :]).then_inc(q_rounded, 1)

            def normalise(b, s):
                wait(pool, o_sum_done, b * 2 + 2)
                wait(pool, tr_done, b - 1)
                pool.tensor_tensor(o_nrm[:, s, :, :], o_sum[:, s, :, :],
                                   rden[:, s, :].unsqueeze(2).to_broadcast([P, NH, HD]), ALU.mult
                                   ).then_inc(o_nrm_done, 1)
            load_q(0, 0)
            load_q(1, 1)
            round_q(0, 0)
            round_q(1, 1)

            def body(b, s, kbs, nxt):
                if not isinstance(b, int) or b + 2 < NB:
                    load_q(b + 2, s)
                if not isinstance(b, int) or b > 0:
                    normalise(b - 1, 1 - s)
                if not isinstance(b, int) or b + 2 < NB:
                    round_q(b + 2, s)
            blocks(pool, body)
            normalise(NB - 1, (NB - 1) % 2)

        @block.vector
        def _(dve):
            dve.wait_ge(const_in, 48)
            dve.tensor_scalar(neg_sink[:], snk[:], -1.0, None, ALU.mult)
            for g in range(NG):
                tok = slice(g * GRP, (g + 1) * GRP)
                dve.wait_ge(k_rounded, 2 * g + 2)
                dve.tensor_tensor(kb[0:HD, :, tok], k_raw[0:HD, :, :], kb[0:HD, :, tok].bitcast(F32),
                                  ALU.subtract).then_inc(k_split, 1)
                dve.tensor_tensor(ka[HD:P, :, tok], k_raw[HD:P, :, :], ka[HD:P, :, tok].bitcast(F32),
                                  ALU.subtract).then_inc(k_split, 1)
            dve.wait_ge(v_hi_done, 1)
            dve.tensor_tensor(vv[:, :, :, 1, :], v_raw[:], vv[:, :, :, 0, :].bitcast(F32), ALU.subtract
                              ).then_inc(v_split, 1)

            def rest_q(b, s):
                dve.wait_ge(q_rounded, b + 1)
                dve.tensor_tensor(qs[HD:P, s, :, :], q_raw[HD:P, s, :, :], qs[HD:P, s, :, :].bitcast(F32),
                                  ALU.subtract).then_inc(q_split, 1)

            def add_bias(b, s, h, kbs):
                w = len(kbs) * P
                wait(dve, pt_done, b * NH + h - 3)
                dve.wait_ge(sc_done, b * NH + h + 1)
                dve.sem_inc(passed_dve, 1)
                dve.tensor_tensor_reduce(prob[:, h % 4, 0:w], sc[:, h % 2, 0:w],
                                         bias[:, h, kbs[0] * P:kbs[0] * P + w], 1.0, neg_sink[:, h:h + 1],
                                         ALU.add, ALU.min, nmax[:, s, h:h + 1]).then_inc(biased, 1)

            def rest_p(b, h, kbs):
                w = len(kbs) * P
                dve.wait_ge(pt_hi_done, b * NH + h + 1)
                dve.tensor_tensor(pt_lo[:, h % 2, 0:w], pt[:, h % 2, 0:w], pt_hi[:, h % 2, 0:w].bitcast(F32),
                                  ALU.subtract).then_inc(pt_split, 1)

            def denominators(b, s):
                dve.wait_ge(sink_exp, b + 1)
                dve.tensor_tensor(den[:, s, :], esum[:, s, :], esink[:, s, :], ALU.add)
                dve.drain()
                dve.reciprocal(rden[:, s, :], den[:, s, :])

            def sum_half(b, s, half):
                hs = slice(half * 4, half * 4 + 4)
                wait(dve, o_nrm_done, b - 1)
                dve.wait_ge(o_lo_done, b * 2 + (half + 1))
                dve.tensor_tensor(o_sum[:, s, hs, :], pv[:, half, :, 0:HD], o_lo[:, s, hs, :], ALU.add
                                  ).then_inc(o_sum_done, 1)

            def finish(b, s):
                denominators(b, s)
                sum_half(b, s, 1)

            dve.drain()
            rest_q(0, 0)
            add_bias(0, 0, 0, window(0))
            add_bias(0, 0, 1, window(0))

            def body(b, s, kbs, nxt):
                for h in range(NH):
                    nx = ahead(b, s, h, kbs, nxt)
                    if nx:
                        add_bias(*nx)
                    rest_p(b, h, kbs)
                    if h == 0 and not (isinstance(b, int) and b == 0):
                        finish(b - 1, 1 - s)
                    if h == 2 and nxt:
                        rest_q(b + 1, 1 - s)
                    if h == 5:
                        sum_half(b, s, 0)
                dve.drain()
                dve.tensor_tensor(esink[:, s, :], nmax[:, s, :], neg_sink[:], ALU.subtract
                                  ).then_inc(sink_arg, 1)
            blocks(dve, body)
            finish(NB - 1, (NB - 1) % 2)

        @block.scalar
        def _(act):
            for g in range(NG):
                tok = slice(g * GRP, (g + 1) * GRP)
                act.wait_ge(k_ld, 32 * g + 32)
                act.copy(ka[:, :, tok], k_raw[:]).then_inc(k_rounded, 1)
                act.copy(kb[:, :, tok], k_raw[:]).then_inc(k_rounded, 1)
            act.wait_ge(v_ld, 16)
            act.copy(vv[:, :, :, 0, :], v_raw[:]).then_inc(v_hi_done, 1)

            def exponentials(b, s, h, kbs):
                w = len(kbs) * P
                act.wait_ge(biased, b * NH + h + 1)
                act.activation(prob[:, h % 4, 0:w], prob[:, h % 4, 0:w], ACT.Exp, bias=nmax[:, s, h:h + 1],
                               scale=-1.0, accum_out=esum[:, s, h:h + 1]).then_inc(exp_done, 1)

            def high_p(b, h, kbs):
                w = len(kbs) * P
                wait(act, pv_done, b * NH + h - 1)
                act.wait_ge(pt_done, b * NH + h + 1)
                act.copy(pt_hi[:, h % 2, 0:w], pt[:, h % 2, 0:w]).then_inc(pt_hi_done, 1)

            def low_half(b, s, half):
                hs = slice(half * 4, half * 4 + 4)
                wait(act, o_sum_done, b * 2 - 2)
                act.wait_ge(pv_done, b * NH + (half * 4 + 4))
                act.copy(o_lo[:, s, hs, :], pv[:, half, :, HD:P]).then_inc(o_lo_done, 1)

            def sinks(b, s):
                act.wait_ge(sink_arg, b + 1)
                act.activation(esink[:, s, :], esink[:, s, :], ACT.Exp).then_inc(sink_exp, 1)

            def outputs(b, s):
                act.wait_ge(tr_done, b + 1)
                wait(act, ot_st[s], (b - s) * 8)
                act.copy(ot[:, s, :, :], tr[:, s, :, :]).then_inc(ot_done, 1)

            exponentials(0, 0, 0, window(0))
            exponentials(0, 0, 1, window(0))

            def body(b, s, kbs, nxt):
                later = not (isinstance(b, int) and b == 0)
                for h in range(NH):
                    nx = ahead(b, s, h, kbs, nxt)
                    if nx:
                        exponentials(*nx)
                    if h == 0 and later:
                        sinks(b - 1, 1 - s)
                    high_p(b, h, kbs)
                    if h == 0 and later:
                        low_half(b - 1, 1 - s, 1)
                    if h == 4:
                        low_half(b, s, 0)
                    if h == 6 and later:
                        outputs(b - 1, 1 - s)
            blocks(act, body)
            sinks(NB - 1, (NB - 1) % 2)
            low_half(NB - 1, (NB - 1) % 2, 1)
            outputs(NB - 1, (NB - 1) % 2)

        @block.tensor
        def _(pe):
            def scores(b, s, h, kbs):
                w = len(kbs) * P
                wait(pe, biased, b * NH + h - 1)
                if h == 0:
                    pe.wait_ge(q_split, b + 1)
                out, keys = sc[:, h % 2, 0:w], bass.ds((b + (kbs[0] - 1)) * P, w)
                pe.matmul(out, qs[:, s, h, :], kb[:, h // QPK, keys], start=True, stop=False)
                pe.matmul(out, qs[:, s, h, :], ka[:, h // QPK, keys], start=False, stop=True
                          ).then_inc(sc_done, 1)

            def turn(b, h, kbs):
                wait(pe, pt_split, b * NH + h - 1)
                pe.wait_ge(exp_done, b * NH + h + 1)
                for i in range(len(kbs)):
                    mm = pe.transpose(pt[:, h % 2, i * P:(i + 1) * P], prob[:, h % 4, i * P:(i + 1) * P],
                                      ident[:])
                mm.then_inc(pt_done, 1)

            def values(b, s, h, kbs):
                if h % 4 == 0:
                    wait(pe, o_sum_done, b * 2 + (h // 4 - 1))
                pe.wait_ge(pt_split, b * NH + h + 1)
                for i, kb_ in enumerate(kbs):
                    keys = vv[:, bass.ds(b + (kb_ - 1), 1), h // QPK, :, :]
                    for half, p in enumerate((pt_lo, pt_hi)):
                        mm = pe.matmul(pv[:, h // 4, h % 4, :], p[:, h % 2, i * P:(i + 1) * P], keys,
                                       start=i + half == 0, stop=i == len(kbs) - 1 and half == 1)
                mm.then_inc(pv_done, 1)

            def outputs(b, s):
                wait(pe, ot_done, b - 1)
                pe.wait_ge(o_nrm_done, b + 1)
                flat = o_nrm[:, s, :, :].rearrange("p h d -> p (h d)")
                for i in range(4):
                    mm = pe.transpose(tr[:, s, i, :], flat[:, i * P:(i + 1) * P], ident[:])
                mm.then_inc(tr_done, 1)

            pe.wait_ge(const_in, 48)
            pe.wait_ge(k_split, 2 * NG)
            pe.wait_ge(v_split, 1)
            scores(0, 0, 0, window(0))
            scores(0, 0, 1, window(0))

            def body(b, s, kbs, nxt):
                for h in range(NH):
                    nx = ahead(b, s, h, kbs, nxt)
                    if nx:
                        scores(*nx)
                    if h:
                        values(b, s, h - 1, kbs)
                    turn(b, h, kbs)
                    if h == 4 and not (isinstance(b, int) and b == 0):
                        outputs(b - 1, 1 - s)
                values(b, s, NH - 1, kbs)
            blocks(pe, body)
            outputs(NB - 1, (NB - 1) % 2)


def shape_constants():
    out = {"ident": np.eye(P, dtype=np.float32)}
    arg = 2 * np.pi * (np.outer(np.arange(P), np.arange(P)) % P) / P
    out["chan"] = np.stack([np.cos(arg), np.sin(arg)], axis=1).astype(np.float64) / math.sqrt(P)
    for i, (_, n) in enumerate(SEQS):
        ne, no, w, ch = slices(n)
        s, t = np.arange(ne * P)[:, None], np.arange(ch * w)[None, :]
        arg = 2 * np.pi * (s * t % n) / n
        out[f"table{i}"] = np.concatenate([np.cos(arg) * (s <= n // 2), np.sin(arg)[:no * P]], 0) / math.sqrt(n)
    rel = np.arange(3 * P)[None, :] - P - np.arange(P)[:, None]
    slope = 2.0 ** (-8.0 * (np.arange(NH) + 1) / NH)
    dist = np.abs(rel)
    out["bias"] = np.where(dist[:, None, :] <= P, slope[None, :, None] * dist[:, None, :], BIG)
    return {k: v.astype(np.float32) for k, v in out.items()}


def mix_out(nc, xn_d, heads_d, w_out, ln_g, ln_b, ident_d, x1_d, x1t_d):
    with ExitStack() as ctx:
        al = Phase(nc, ctx, "d")
        ident = al.sb("ident", [P, P])
        gain = al.sb("gain", [P, D])
        shift = al.sb("shift", [P, D])
        eps = al.sb("eps", [P, 1])
        mhalf = al.sb("mhalf", [P, 1])
        w_raw = al.sb("w_raw", [P, 2, D])
        w_hi = al.sb("w_hi", [P, KT, D], F32R)
        w_lo = al.sb("w_lo", [P, KT, D], F32R)
        h_raw = al.sb("h_raw", [P, 2, KT, P])
        h_hi = al.sb("h_hi", [P, 2, KT, P], F32R)
        h_lo = al.sb("h_lo", [P, 2, KT, P], F32R)
        xn = al.sb("xn", [P, 2, D])
        y = al.sb("y", [P, 2, D])
        yg = al.sb("yg", [P, 2, D])
        x1 = al.sb("x1", [P, 2, D])
        x1t = al.sb("x1t", [P, 2, KT, P])
        stats = al.sb("stats", [P, 2, 2, 6])
        mv = al.sb("mv", [P, 2, 2])
        var_eps = al.sb("var_eps", [P, 2])
        rstd = al.sb("rstd", [P, 2])
        mix = al.ps("mix", [P, 2, 2, 512])
        turn = al.ps("turn", [P, 2, 2, 512])

        const_in, const_set = al.sem("const_in"), al.sem("const_set")
        w_ld, w_hi_done, w_split = al.sems("w_ld", 2), al.sem("w_hi_done"), al.sem("w_split")
        h_ld, h_hi_done, h_split = al.sems("h_ld", 2), al.sem("h_hi_done"), al.sem("h_split")
        xn_ld, mix_done, y_done = al.sems("xn_ld", 2), al.sem("mix_done"), al.sem("y_done")
        stats_done, var_done, rstd_done = al.sem("stats_done"), al.sem("var_done"), al.sem("rstd_done")
        passed = al.sem("passed")
        x1_done, x1_st = al.sem("x1_done"), al.sems("x1_st", 2)
        turned, x1t_done, x1t_st = al.sem("turned"), al.sem("x1t_done"), al.sems("x1t_st", 2)

        heads_v = heads_d.rearrange("(k p) t -> p k t", p=P)
        x1t_v = x1t_d.rearrange("(k p) t -> p k t", p=P)
        block = ctx.enter_context(nc.Block())

        def tiles(eng, body):
            for s in range(2):
                body(s, s, True)
            with eng.Fori(1, NT // 2) as i:
                for s in range(2):
                    body(i * 2 + s, s, False)

        @block.sync
        def _(sp):
            sp.dma_start(gain[:], ln_g.partition_broadcast(P)).then_inc(const_in, 16)
            sp.dma_start(shift[:], ln_b.partition_broadcast(P)).then_inc(const_in, 16)
            sp.dma_start(ident[:], ident_d).then_inc(const_in, 16)
            for k in range(KT):
                if k >= 2:
                    sp.wait_ge(w_split, k - 1)
                sp.dma_start(w_raw[:, k % 2, :], w_out[k * P:(k + 1) * P, :]).then_inc(w_ld[k % 2], 16)

            def store(n, s, first):
                sp.wait_ge(x1_done, n + 1)
                sp.dma_start(x1_d[bass.ds(n * P, P), :], x1[:, s, :]).then_inc(x1_st[s], 16)
                sp.wait_ge(x1t_done, n + 1)
                sp.sem_inc(passed, 1)
                sp.dma_start(x1t_v[:, :, bass.ds(n * P, P)], x1t[:, s, :, :]).then_inc(x1t_st[s], 16)
            tiles(sp, store)
            for s in range(2):
                sp.wait_ge(x1_st[s], 16 * (NT // 2))
                sp.wait_ge(x1t_st[s], 16 * (NT // 2))

        @block.gpsimd
        def _(pool):
            def load(n, s, first):
                if not first:
                    pool.wait_ge(h_split, n - 1)
                pool.dma_start(h_raw[:, s, :, :], heads_v[:, :, bass.ds(n * P, P)]).then_inc(h_ld[s], 16)
                if not first:
                    pool.wait_ge(y_done, n - 1)
                pool.dma_start(xn[:, s, :], xn_d[bass.ds(n * P, P), :]).then_inc(xn_ld[s], 16)

            def inverse_std(n, s):
                pool.wait_ge(stats_done, n + 1)
                pool.tensor_tensor(var_eps[:, s:s + 1], mv[:, s, 1:2], eps[:], ALU.add).then_inc(var_done, 1)
                pool.wait_ge(var_done, n + 1)
                pool.tensor_tensor(rstd[:, s:s + 1], var_eps[:, s:s + 1], mhalf[:], ALU.pow
                                   ).then_inc(rstd_done, 1)
            load(0, 0, True)
            load(1, 1, True)
            pool.memset(eps[:], EPS).then_inc(const_set, 1)
            pool.memset(mhalf[:], -0.5).then_inc(const_set, 1)
            for k in range(KT):
                pool.wait_ge(w_hi_done, k + 1)
                pool.tensor_tensor(w_lo[:, k, :], w_raw[:, k % 2, :], w_hi[:, k, :].bitcast(F32),
                                   ALU.subtract).then_inc(w_split, 1)
            pool.wait_ge(const_set, 2)
            with pool.Fori(0, NT // 2 - 1) as i:
                for s in range(2):
                    inverse_std(i * 2 + s, s)
                    load(i * 2 + s + 2, s, False)
            for s in range(2):
                inverse_std(NT - 2 + s, s)

        @block.scalar
        def _(act):
            def split_heads(n, s, first):
                act.wait_ge(h_ld[s], (n - s) * 8 + 16)
                if not first:
                    act.wait_ge(mix_done, n - 1)
                act.copy(h_hi[:, s, :, :], h_raw[:, s, :, :]).then_inc(h_hi_done, 1)

            def evacuate_turned(n, s, first):
                act.wait_ge(turned, n + 1)
                if not first:
                    act.wait_ge(x1t_st[s], (n - s) * 8)
                act.copy(x1t[:, s, :, :].rearrange("p k c -> p (k c)"),
                         turn[:, s, :, :].rearrange("p a c -> p (a c)")).then_inc(x1t_done, 1)
            split_heads(0, 0, True)
            split_heads(1, 1, True)
            for k in range(KT):
                act.wait_ge(w_ld[k % 2], 16 * (k // 2 + 1))
                act.copy(w_hi[:, k, :], w_raw[:, k % 2, :]).then_inc(w_hi_done, 1)
            split_heads(2, 0, False)
            evacuate_turned(0, 0, True)
            split_heads(3, 1, False)
            evacuate_turned(1, 1, True)
            with act.Fori(1, NT // 2 - 1) as i:
                for s in range(2):
                    split_heads(i * 2 + s + 2, s, False)
                    evacuate_turned(i * 2 + s, s, False)
            for s in range(2):
                evacuate_turned(NT - 2 + s, s, False)

        @block.vector
        def _(dve):
            def rest_of_heads(n, s):
                dve.wait_ge(h_hi_done, n + 1)
                dve.tensor_tensor(h_lo[:, s, :, :], h_raw[:, s, :, :], h_hi[:, s, :, :].bitcast(F32),
                                  ALU.subtract).then_inc(h_split, 1)

            def norm(n, s, first):
                dve.wait_ge(mix_done, n + 1)
                dve.wait_ge(xn_ld[s], (n - s) * 8 + 16)
                for h in range(2):
                    cols = slice(h * 512, (h + 1) * 512)
                    add = dve.scalar_tensor_tensor(y[:, s, cols], xn[:, s, cols], ALPHA, mix[:, s, h, :],
                                                   ALU.mult, ALU.add)
                add.then_inc(y_done, 1)
                dve.drain()
                for h in range(2):
                    dve.bn_stats(stats[:, s, h, :], y[:, s, h * 512:(h + 1) * 512])
                dve.drain()
                dve.bn_aggr(mv[:, s, :], stats[:, s, :, :]).then_inc(stats_done, 1)
                dve.drain()
                if first and s == 0:
                    dve.wait_ge(const_in, 48)
                dve.scalar_tensor_tensor(yg[:, s, :], y[:, s, :], mv[:, s, 0:1], gain[:], ALU.subtract,
                                         ALU.mult)
                dve.drain()
                dve.wait_ge(rstd_done, n + 1)
                if not first:
                    dve.wait_ge(turned, n - 1)
                    dve.wait_ge(x1_st[s], (n - s) * 8)
                dve.scalar_tensor_tensor(x1[:, s, :], yg[:, s, :], rstd[:, s:s + 1], shift[:], ALU.mult,
                                         ALU.add).then_inc(x1_done, 1)
            rest_of_heads(0, 0)
            rest_of_heads(1, 1)
            for s in range(2):
                norm(s, s, True)
                rest_of_heads(s + 2, s)
            with dve.Fori(1, NT // 2 - 1) as i:
                for s in range(2):
                    norm(i * 2 + s, s, False)
                    rest_of_heads(i * 2 + s + 2, s)
            for s in range(2):
                norm(NT - 2 + s, s, False)

        @block.tensor
        def _(pe):
            def product(n, s, first):
                for h in range(2):
                    cols = slice(h * 512, (h + 1) * 512)
                    for k in range(KT):
                        if h == 0 and k == 0:
                            pe.wait_ge(h_split, n + 1)
                            if not first:
                                pe.wait_ge(y_done, n - 1)
                        if first and h == 0 and s == 0:
                            pe.wait_ge(w_split, k + 1)
                        mm = split_mm(pe, mix[:, s, h, :], h_hi[:, s, k, :], h_lo[:, s, k, :],
                                      w_hi[:, k, cols], w_lo[:, k, cols], k == 0, k == KT - 1)
                mm.then_inc(mix_done, 1)

            def transpose(n, s, first):
                for k in range(KT):
                    if k == 0:
                        pe.wait_ge(x1_done, n + 1)
                        if not first:
                            pe.wait_ge(x1t_done, n - 1)
                    mm = pe.transpose(turn[:, s, k // 4, (k % 4) * P:(k % 4 + 1) * P],
                                      x1[:, s, k * P:(k + 1) * P], ident[:])
                mm.then_inc(turned, 1)
            pe.wait_ge(const_in, 48)
            product(0, 0, True)
            product(1, 1, True)
            product(2, 0, False)
            transpose(0, 0, True)
            product(3, 1, False)
            transpose(1, 1, True)
            with pe.Fori(1, NT // 2 - 1) as i:
                for s in range(2):
                    product(i * 2 + s + 2, s, False)
                    transpose(i * 2 + s, s, False)
            for s in range(2):
                transpose(NT - 2 + s, s, False)


def mlp(nc, x1_d, x1t_d, w1_d, w2_d, ln_g, ln_b, out_d):
    UC = 8
    NC = FF // (UC * P)
    with ExitStack() as ctx:
        al = Phase(nc, ctx, "e")
        gain = al.sb("gain", [P, D])
        shift = al.sb("shift", [P, D])
        eps = al.sb("eps", [P, TPG])
        mhalf = al.sb("mhalf", [P, TPG])
        xt_raw = al.sb("xt_raw", [P, 2, GRP])
        xt_hi = al.sb("xt_hi", [P, KT, GRP], F32R)
        xt_lo = al.sb("xt_lo", [P, KT, GRP], F32R)
        w1_raw = al.sb("w1_raw", [P, 2, KT * P])
        w1_hi = al.sb("w1_hi", [P, 2, KT * P], F32R)
        w1_lo = al.sb("w1_lo", [P, 2, KT * P], F32R)
        w2_raw = al.sb("w2_raw", [P, 2, D])
        w2_hi = al.sb("w2_hi", [P, UC, D], F32R)
        w2_lo = al.sb("w2_lo", [P, UC, D], F32R)
        relu = al.sb("relu", [P, 4, GRP])
        hid = al.sb("hid", [P, 2, GRP])
        h_hi = al.sb("h_hi", [P, UC, GRP], F32R)
        h_lo = al.sb("h_lo", [P, UC, GRP], F32R)
        acc = al.sb("acc", [P, TPG, D])
        stats = al.sb("stats", [P, TPG, 2, 6])
        mv = al.sb("mv", [P, TPG, 2])
        var_eps = al.sb("var_eps", [P, TPG])
        rstd = al.sb("rstd", [P, TPG])
        up = al.ps("up", [P, 4, 512])
        down = al.ps("down", [P, 4, 512])

        const_in, const_set = al.sem("const_in"), al.sem("const_set")
        xt_ld, xt_hi_done, xt_split = al.sems("xt_ld", 2), al.sem("xt_hi_done"), al.sem("xt_split")
        w1_ld, w1_hi_done, w1_split = al.sems("w1_ld", 2), al.sem("w1_hi_done"), al.sem("w1_split")
        w2_ld, w2_hi_done, w2_split = al.sems("w2_ld", 2), al.sem("w2_hi_done"), al.sem("w2_split")
        up_done, relu_done, h_hi_done = al.sem("up_done"), al.sem("relu_done"), al.sem("h_hi_done")
        h_split = al.sem("h_split")
        down_done, down_read = al.sem("down_done"), al.sem("down_read")
        x1_ld = al.sems("x1_ld", TPG)
        stats_done, var_done, rstd_done = al.sem("stats_done"), al.sem("var_done"), al.sem("rstd_done")
        y_done, y_st = al.sem("y_done"), al.sems("y_st", TPG)

        block = ctx.enter_context(nc.Block())


        @block.sync
        def _(sp):
            def store_y(g):
                for t in range(TPG):
                    sp.wait_ge(y_done, g * TPG + t + 1)
                    sp.dma_start(out_d[bass.ds(g * GRP + t * P, P), :], acc[:, t, :]).then_inc(y_st[t], 16)

            def load_weights(g, c, u):
                sp.wait_ge(w1_split, (g * NC + c) * UC + u + 1)
                sp.dma_start(w1_raw[:, u % 2, :], w1_d[bass.ds((c * UC + u) * P, P), :]
                             ).then_inc(w1_ld[u % 2], 16)
                sp.wait_ge(w2_split, (g * NC + c) * UC + u + 1)
                sp.dma_start(w2_raw[:, u % 2, :], w2_d[bass.ds((c * UC + u) * P, P), :]
                             ).then_inc(w2_ld[u % 2], 16)

            def group(g, first):
                for k in range(KT):
                    sp.wait_ge(xt_split, g * KT + k + 1)
                    sp.dma_start(xt_raw[:, k % 2, :], x1t_d[k * P:(k + 1) * P, bass.ds(g * GRP, GRP)]
                                 ).then_inc(xt_ld[k % 2], 16)
                for u in range(UC):
                    load_weights(g, 0, u)
                    if u == 4 and not first:
                        store_y(g - 1)
                    if u == 5:
                        for t in range(TPG):
                            if not first:
                                sp.wait_ge(y_st[t], g * 16)
                            sp.dma_start(acc[:, t, :], x1_d[bass.ds(g * GRP + t * P, P), :]
                                         ).then_inc(x1_ld[t], 16)
                with sp.Fori(1, NC) as c:
                    for u in range(UC):
                        load_weights(g, c, u)

            sp.dma_start(gain[:], ln_g.partition_broadcast(P)).then_inc(const_in, 16)
            sp.dma_start(shift[:], ln_b.partition_broadcast(P)).then_inc(const_in, 16)
            group(0, True)
            with sp.Fori(1, NG) as g:
                group(g, False)
            store_y(NG - 1)
            for t in range(TPG):
                sp.wait_ge(y_st[t], NG * 16)

        @block.gpsimd
        def _(pool):
            def x1_lows(g):
                for k in range(KT):
                    pool.wait_ge(xt_hi_done, g * KT + k + 1)
                    pool.tensor_tensor(xt_lo[:, k, :], xt_raw[:, k % 2, :], xt_hi[:, k, :].bitcast(F32),
                                       ALU.subtract).then_inc(xt_split, 1)

            def w1_lows(cc, units):
                for u in units:
                    pool.wait_ge(w1_hi_done, cc * UC + u + 1)
                    pool.tensor_tensor(w1_lo[:, u % 2, :], w1_raw[:, u % 2, :],
                                       w1_hi[:, u % 2, :].bitcast(F32), ALU.subtract).then_inc(w1_split, 1)

            def inverse_std(g):
                pool.wait_ge(stats_done, g * TPG + TPG)
                pool.tensor_tensor(var_eps[:], mv[:, :, 1], eps[:], ALU.add).then_inc(var_done, 1)
                pool.wait_ge(var_done, g + 1)
                pool.tensor_tensor(rstd[:], var_eps[:], mhalf[:], ALU.pow).then_inc(rstd_done, 1)

            def later_chunks(g):
                with pool.Fori(1, NC) as c:
                    w1_lows(g * NC + c, range(UC))

            pool.sem_inc(xt_split, 2)
            pool.sem_inc(w1_split, 2)
            pool.memset(eps[:], EPS).then_inc(const_set, 1)
            pool.memset(mhalf[:], -0.5).then_inc(const_set, 1)
            x1_lows(0)
            w1_lows(0, range(UC))
            later_chunks(0)
            pool.wait_ge(const_set, 2)
            with pool.Fori(1, NG) as g:
                x1_lows(g)
                w1_lows(g * NC, range(2))
                inverse_std(g - 1)
                w1_lows(g * NC, range(2, UC))
                later_chunks(g)
            inverse_std(NG - 1)

        @block.scalar
        def _(act):
            act.sem_inc(relu_done, 4)
            with act.Fori(0, NG) as g:
                for k in range(KT):
                    act.wait_ge(xt_ld[k % 2], g * (KT * 8) + (k // 2) * 16 + 16)
                    act.wait_ge(up_done, g * (NC * UC) + 2)
                    act.copy(xt_hi[:, k, :], xt_raw[:, k % 2, :]).then_inc(xt_hi_done, 1)
                with act.Fori(0, NC) as c:
                    n = (g * NC + c) * UC

                    def w1_high(u):
                        act.wait_ge(w1_ld[u % 2], n * 8 + (u // 2) * 16 + 16)
                        act.wait_ge(up_done, n + u + 1)
                        act.copy(w1_hi[:, u % 2, :], w1_raw[:, u % 2, :]).then_inc(w1_hi_done, 1)

                    w1_high(0)
                    w1_high(1)
                    for u in range(UC):
                        if u + 2 < UC:
                            w1_high(u + 2)
                        act.wait_ge(up_done, n + u + 3)
                        act.wait_ge(h_split, n + u + 1)
                        act.activation(relu[:, u % 4, :], up[:, u % 4, :], ACT.Relu).then_inc(relu_done, 1)
                        act.wait_ge(relu_done, n + u + 5)
                        act.wait_ge(down_done, n + 1)
                        act.activation(h_hi[:, u, :], relu[:, u % 4, :], ACT.Square).then_inc(h_hi_done, 1)
                        act.wait_ge(w2_ld[u % 2], n * 8 + (u // 2) * 16 + 16)
                        act.copy(w2_hi[:, u, :], w2_raw[:, u % 2, :]).then_inc(w2_hi_done, 1)

        @block.vector
        def _(dve):
            def chunk(g, c, start, end):
                n = (g * NC + c) * UC
                for u in range(UC):
                    dve.wait_ge(relu_done, n + u + 5)
                    dve.tensor_tensor(hid[:, u % 2, :], relu[:, u % 4, :], relu[:, u % 4, :], ALU.mult)
                    dve.drain()
                    dve.wait_ge(h_hi_done, n + u + 1)
                    dve.tensor_tensor(h_lo[:, u, :], hid[:, u % 2, :], h_hi[:, u, :].bitcast(F32),
                                      ALU.subtract).then_inc(h_split, 1)
                    dve.wait_ge(w2_hi_done, n + u + 1)
                    dve.tensor_tensor(w2_lo[:, u, :], w2_raw[:, u % 2, :], w2_hi[:, u, :].bitcast(F32),
                                      ALU.subtract).then_inc(w2_split, 1)
                if start:
                    for t in range(TPG):
                        dve.wait_ge(x1_ld[t], g * 16 + 16)
                        dve.tensor_scalar(acc[:, t, :], acc[:, t, :], ALPHA, None, ALU.mult)
                    dve.drain()
                for o in range(2 * TPG):
                    t, cols = o // 2, slice((o % 2) * 512, (o % 2 + 1) * 512)
                    dve.wait_ge(down_done, n + o + 2)
                    dve.tensor_tensor(acc[:, t, cols], down[:, o % 4, :], acc[:, t, cols], ALU.add
                                      ).then_inc(down_read, 1)
                    if end and o % 2:
                        dve.drain()
                        for h in range(2):
                            dve.bn_stats(stats[:, t, h, :], acc[:, t, h * 512:(h + 1) * 512])

            def norm(g):
                dve.drain()
                for t in range(TPG):
                    dve.bn_aggr(mv[:, t, :], stats[:, t, :, :]).then_inc(stats_done, 1)
                dve.drain()
                for t in range(TPG):
                    dve.scalar_tensor_tensor(acc[:, t, :], acc[:, t, :], mv[:, t, 0:1], gain[:],
                                             ALU.subtract, ALU.mult)
                dve.drain()
                for t in range(TPG):
                    dve.wait_ge(rstd_done, g + 1)
                    dve.scalar_tensor_tensor(acc[:, t, :], acc[:, t, :], rstd[:, t:t + 1], shift[:],
                                             ALU.mult, ALU.add).then_inc(y_done, 1)

            dve.sem_inc(h_split, 4)
            dve.sem_inc(w2_split, 2)
            dve.sem_inc(down_read, 4)
            dve.wait_ge(const_in, 32)
            with dve.Fori(0, NG) as g:
                chunk(g, 0, True, False)
                with dve.Fori(1, NC - 1) as c:
                    chunk(g, c, False, False)
                chunk(g, NC - 1, False, True)
                norm(g)

        @block.tensor
        def _(pe):
            pe.sem_inc(up_done, 2)
            pe.sem_inc(down_done, 1)
            with pe.Fori(0, NG) as g:
                with pe.Fori(0, NC) as c:
                    n = (g * NC + c) * UC
                    for u in range(UC):
                        for k in range(KT):
                            if u == 0:
                                pe.wait_ge(xt_split, g * KT + k + 3)
                            if k == 0:
                                pe.wait_ge(w1_split, n + u + 3)
                                pe.wait_ge(relu_done, n + u + 1)
                            cols = slice(k * P, (k + 1) * P)
                            mm = split_mm(pe, up[:, u % 4, :], w1_hi[:, u % 2, cols], w1_lo[:, u % 2, cols],
                                          xt_hi[:, k, :], xt_lo[:, k, :], k == 0, k == KT - 1)
                        mm.then_inc(up_done, 1)
                    for o in range(2 * TPG):
                        tok = slice((o // 2) * P, (o // 2 + 1) * P)
                        cols = slice((o % 2) * 512, (o % 2 + 1) * 512)
                        for k in range(UC):
                            if o == 0:
                                pe.wait_ge(h_split, n + k + 5)
                                pe.wait_ge(w2_split, n + k + 3)
                            if k == 0:
                                pe.wait_ge(down_read, n + o + 1)
                            mm = split_mm(pe, down[:, o % 4, :], h_hi[:, k, tok], h_lo[:, k, tok],
                                          w2_hi[:, k, cols], w2_lo[:, k, cols], k == 0, k == UC - 1)
                        mm.then_inc(down_done, 1)



def build(nc, d, s, y):
    embed_project(nc, d["x"], d["ln_emb_g"], d["ln_emb_b"], d["w_in"], d["ident"], s["x_norm"], s["proj"],
                  s["v"])
    for i, (tok0, seq_len) in enumerate(SEQS):
        fourier(nc, f"b{i}", tok0, seq_len, s["proj"], d["w_fourier"], d["chan"], d[f"table{i}"], s["heads"])
    attend(nc, s["proj"], s["v"], d["sink"], d["bias"], d["ident"], s["heads"])
    mix_out(nc, s["x_norm"], s["heads"], d["w_out"], d["ln_mix_g"], d["ln_mix_b"], d["ident"], s["x1"], s["x1t"])
    mlp(nc, s["x1"], s["x1t"], d["w_ff1"], d["w_ff2"], d["ln_ffn_g"], d["ln_ffn_b"], y)


def kernel(x_prompt, x_sample, ln_emb_g, ln_emb_b, w_in, w_fourier, sink_logits, w_out, ln_mix_g, ln_mix_b,
           w_ff1, w_ff2, ln_ffn_g, ln_ffn_b):
    import concourse.bacc as bacc
    from concourse.bass_utils import run_bass_kernel_spmd
    nc = bacc.Bacc("TRN2", target_bir_lowering=False, num_devices=1)
    host = {
        "x": np.concatenate([np.asarray(x_prompt)[0], np.asarray(x_sample)[0]], axis=0),
        "ln_emb_g": ln_emb_g, "ln_emb_b": ln_emb_b,
        "w_in": np.asarray(w_in)[0], "w_fourier": np.asarray(w_fourier)[0], "sink": np.asarray(sink_logits)[0],
        "w_out": np.asarray(w_out)[0], "ln_mix_g": np.asarray(ln_mix_g)[0], "ln_mix_b": np.asarray(ln_mix_b)[0],
        "w_ff1": np.asarray(w_ff1)[0].reshape(KT, P, FF // P, P).transpose(2, 1, 0, 3).reshape(FF, D),
        "w_ff2": np.asarray(w_ff2)[0], "ln_ffn_g": np.asarray(ln_ffn_g)[0], "ln_ffn_b": np.asarray(ln_ffn_b)[0],
        **shape_constants(),
    }
    host = {k: np.ascontiguousarray(v) for k, v in host.items()}
    d = {k: nc.dram_tensor(k, v.shape, F32, kind="ExternalInput").ap() for k, v in host.items()}
    scratch = {"x_norm": (TOK, D), "proj": (FT * P, TOK), "v": (TOK, P), "heads": (D, TOK + 2),
               "x1": (TOK, D), "x1t": (D, TOK)}
    s = {k: nc.dram_tensor(f"s_{k}", shape, F32, kind="Internal").ap() for k, shape in scratch.items()}
    y = nc.dram_tensor("y", (TOK, D), F32, kind="ExternalOutput").ap()
    build(nc, d, s, y)
    got = run_bass_kernel_spmd(nc, [host], core_ids=[0]).results[0]["y"]
    return tuple(got[None, t:t + n] for t, n in SEQS)
```

```python
import math
from contextlib import ExitStack

import numpy as np

import concourse.bass as bass
from concourse import mybir

F32 = mybir.dt.float32
F32R = mybir.dt.float32r
ACT = mybir.ActivationFunctionType
ALU = mybir.AluOpType

P = 128
D = 1024
KT = D // P
SEQS = ((0, 512), (512, 2048))
TOK = sum(s for _, s in SEQS)
GRP = 512
NG = TOK // GRP
TPG = GRP // P
NT = TOK // P
FOUR = 512
NFG = 4
HD = 64
NH = 8
NKV = 2
QPK = NH // NKV
IN_W = FOUR + NH * HD + 2 * NKV * HD
KROW = FOUR + NH * HD
FT = KROW // P + 1
FF = 4 * D
EPS = 1e-5
ALPHA = 2.0 ** 0.25
QSCALE = -1.0 / math.sqrt(HD)
BIG = 1e30


def slices(seq_len):
    half = seq_len // 2
    chunks = -(-(half + 1) // 512)
    width = -(-(half + 1) // chunks)
    width += width % 2
    return half // P + 1, half // P, width, chunks


def split_mm(tensor, out, w_hi, w_lo, m_hi, m_lo, first, last):
    tensor.matmul(out, w_lo, m_hi, start=first, stop=False)
    tensor.matmul(out, w_hi, m_lo, start=False, stop=False)
    return tensor.matmul(out, w_hi, m_hi, start=False, stop=last)


class Phase:

    def __init__(self, nc, ctx, phase):
        self.nc, self.ctx, self.phase, self.used = nc, ctx, phase, []
        ctx.callback(self.release)

    def release(self):
        if self.used:
            self.nc.clear_and_free_semaphores(self.used)
            self.nc.all_engine_barrier()

    def sb(self, name, shape, dt=F32):
        return self.ctx.enter_context(self.nc.sbuf_tensor(f"{self.phase}_{name}", shape, dt))

    def ps(self, name, shape):
        return self.ctx.enter_context(self.nc.psum_tensor(f"{self.phase}_{name}", shape, F32))

    def sem(self, name):
        self.used.append(self.nc.alloc_semaphore(f"{self.phase}_{name}"))
        return self.used[-1]

    def sems(self, name, n):
        return [self.sem(f"{name}{i}") for i in range(n)]


def embed_project(nc, x, ln_g, ln_b, w_in, ident_d, xn_d, proj_d, v_d):
    with ExitStack() as ctx:
        al = Phase(nc, ctx, "a")
        ident = al.sb("ident", [P, P])
        gain = al.sb("gain", [P, D])
        shift = al.sb("shift", [P, D])
        w_raw = al.sb("w_raw", [P, 2, IN_W])
        w_hi = al.sb("w_hi", [P, KT, IN_W], F32R)
        w_lo = al.sb("w_lo", [P, KT, IN_W], F32R)
        x_in = al.sb("x_in", [P, TPG, D])
        x_nrm = al.sb("x_nrm", [P, TPG, D])
        xg = al.sb("xg", [P, 2, D])
        stats = al.sb("stats", [P, TPG, 2, 6])
        mv = al.sb("mv", [P, TPG, 2])
        var_eps = al.sb("var_eps", [P, TPG])
        rstd = al.sb("rstd", [P, TPG])
        mhalf = al.sb("mhalf", [P, TPG])
        eps = al.sb("eps", [P, TPG])
        xt_hi = al.sb("xt_hi", [P, KT, GRP], F32R)
        xt_lo = al.sb("xt_lo", [P, KT, GRP], F32R)
        stage = al.sb("stage", [P, 5, GRP])
        bank = al.ps("bank", [P, 8, 512])

        const_in, mhalf_set = al.sem("const_in"), al.sem("mhalf_set")
        w_in_ld, w_hi_done, w_split = al.sems("w_in_ld", 2), al.sem("w_hi_done"), al.sem("w_split")
        x_ld, x_free = al.sems("x_ld", TPG), al.sem("x_free")
        stats_done, var_done, rstd_done = al.sem("stats_done"), al.sem("var_done"), al.sem("rstd_done")
        xn_ready = al.sem("xn_ready")
        xn_st = al.sems("xn_st", TPG)
        turned, xt_hi_done, xt_done = al.sem("turned"), al.sem("xt_hi_done"), al.sem("xt_done")
        proj_done, stage_done = al.sem("proj_done"), al.sem("stage_done")
        stage_st = al.sems("stage_st", 5)
        UNITS = FT + 1

        block = ctx.enter_context(nc.Block())

        @block.sync
        def _(sp):
            sp.dma_start(ident[:], ident_d).then_inc(const_in, 16)
            sp.dma_start(gain[:], ln_g.partition_broadcast(P)).then_inc(const_in, 16)
            sp.dma_start(shift[:], ln_b.partition_broadcast(P)).then_inc(const_in, 16)
            for k in range(KT):
                if k >= 2:
                    sp.wait_ge(w_split, k - 1)
                sp.dma_start(w_raw[:, k % 2, :], w_in[k * P:(k + 1) * P, :]).then_inc(w_in_ld[k % 2], 16)
            with sp.Fori(0, NG) as g:
                for j in range(TPG):
                    sp.wait_ge(xn_ready, g * TPG + j + 1)
                    sp.dma_start(xn_d[bass.ds(g * GRP + j * P, P), :], x_nrm[:, j, :]).then_inc(xn_st[j], 16)
                for m in (1, 0, *range(2, UNITS)):
                    if m:
                        sp.wait_ge(stage_done, g * UNITS + UNITS + m + 1)
                    if m < FT:
                        sp.dma_start(proj_d[m * P:(m + 1) * P, bass.ds(g * GRP, GRP)],
                                     stage[:, m % 5, :]).then_inc(stage_st[m % 5], 16)
                    else:
                        sp.dma_start(v_d[bass.ds(g * GRP, GRP), :].rearrange("(t p) c -> p t c", p=P),
                                     stage[:, m % 5, :].rearrange("p (t c) -> p t c", t=TPG)
                                     ).then_inc(stage_st[m % 5], 16)
            for j in range(TPG):
                sp.wait_ge(xn_st[j], 16 * (NG + 1))
            for s in range(5):
                sp.wait_ge(stage_st[s], 16 * (2 * NG + 1))

        @block.gpsimd
        def _(pool):
            def load_x(g, first):
                for j in range(TPG):
                    if not first:
                        pool.wait_ge(x_free, (g - 1) * TPG + j + 1)
                    pool.dma_start(x_in[:, j, :], x[bass.ds(g * GRP + j * P, P), :]).then_inc(x_ld[j], 16)

            def inverse_std(g):
                pool.wait_ge(stats_done, g * TPG + TPG)
                pool.tensor_tensor(var_eps[:], mv[:, :, 1], eps[:], ALU.add).then_inc(var_done, 1)
                pool.wait_ge(var_done, g + 1)
                pool.tensor_tensor(rstd[:], var_eps[:], mhalf[:], ALU.pow).then_inc(rstd_done, 1)

            load_x(0, True)
            pool.memset(mhalf[:], -0.5).then_inc(mhalf_set, 1)
            pool.memset(eps[:], EPS).then_inc(mhalf_set, 1)
            for k in range(KT):
                pool.wait_ge(w_hi_done, k + 1)
                pool.tensor_tensor(w_lo[:, k, :], w_raw[:, k % 2, :], w_hi[:, k, :].bitcast(F32),
                                   ALU.subtract).then_inc(w_split, 1)
            pool.wait_ge(mhalf_set, 2)
            with pool.Fori(0, NG - 1) as g:
                inverse_std(g)
                load_x(g + 1, False)
            inverse_std(NG - 1)

        @block.vector
        def _(dve):
            with dve.Fori(0, NG) as g:
                for j in range(TPG):
                    dve.wait_ge(x_ld[j], g * 16 + 16)
                    for h in range(2):
                        dve.bn_stats(stats[:, j, h, :], x_in[:, j, h * 512:(h + 1) * 512])
                dve.drain()
                for j in range(TPG):
                    dve.bn_aggr(mv[:, j, :], stats[:, j, :, :]).then_inc(stats_done, 1)
                dve.drain()
                dve.wait_ge(const_in, 48)
                dve.wait_ge(rstd_done, g + 1)
                for j in range(TPG):
                    dve.scalar_tensor_tensor(xg[:, j % 2, :], x_in[:, j, :], mv[:, j, 0:1], gain[:], ALU.subtract,
                                             ALU.mult).then_inc(x_free, 1)
                    dve.drain()
                    dve.wait_ge(turned, g * KT + KT)
                    dve.wait_ge(xn_st[j], g * 16 + 16)
                    dve.scalar_tensor_tensor(x_nrm[:, j, :], xg[:, j % 2, :], rstd[:, j:j + 1], shift[:], ALU.mult,
                                             ALU.add).then_inc(xn_ready, 1)
                for k in range(KT):
                    dve.wait_ge(xt_hi_done, g * KT + k + 1)
                    dve.tensor_tensor(xt_lo[:, k, :], bank[:, k, :], xt_hi[:, k, :].bitcast(F32),
                                      ALU.subtract).then_inc(xt_done, 1)

        @block.scalar
        def _(act):
            for s in range(5):
                act.sem_inc(stage_st[s], 16)
            for j in range(TPG):
                act.sem_inc(xn_st[j], 16)
            act.sem_inc(stage_done, UNITS)
            for k in range(KT):
                act.wait_ge(w_in_ld[k % 2], 16 * (k // 2 + 1))
                act.copy(w_hi[:, k, :], w_raw[:, k % 2, :]).then_inc(w_hi_done, 1)
            with act.Fori(0, NG) as g:
                for k in range(KT):
                    act.wait_ge(turned, g * KT + KT + k + 1)
                    act.copy(xt_hi[:, k, :], bank[:, k, :]).then_inc(xt_hi_done, 1)
                for m in range(UNITS):
                    act.wait_ge(proj_done, g * UNITS + m + 1)
                    act.wait_ge(stage_st[m % 5], g * 32 + (m // 5) * 16 + 16)
                    is_q = FOUR // P <= m < KROW // P
                    act.mul(stage[:, m % 5, :], bank[:, m % 8, :], QSCALE if is_q else 1.0
                            ).then_inc(stage_done, 1)

        @block.tensor
        def _(pe):
            pe.sem_inc(turned, KT)
            pe.wait_ge(const_in, 48)
            with pe.Fori(0, NG) as g:
                for k in range(KT):
                    if k == 0:
                        pe.wait_ge(xn_ready, g * TPG + TPG)
                    pe.wait_ge(stage_done, g * UNITS + (k + 9 if k < UNITS - 8 else k + 1))
                    for j in range(TPG):
                        mm = pe.transpose(bank[:, k, j * P:(j + 1) * P], x_nrm[:, j, k * P:(k + 1) * P],
                                          ident[:])
                    mm.then_inc(turned, 1)
                for m in range(UNITS):
                    out = bank[:, m % 8, :]
                    if m >= 8:
                        pe.wait_ge(stage_done, g * UNITS + UNITS + m - 7)
                    if m < FT:
                        cols = slice(m * P, (m + 1) * P)
                        for k in range(KT):
                            if m == 0:
                                pe.wait_ge(w_split, k + 1)
                                pe.wait_ge(xt_done, g * KT + k + 1)
                            mm = split_mm(pe, out, w_hi[:, k, cols], w_lo[:, k, cols], xt_hi[:, k, :],
                                          xt_lo[:, k, :], k == 0, k == KT - 1)
                    else:
                        cols = slice(m * P, (m + 1) * P)
                        for t in range(TPG):
                            tok = slice(t * P, (t + 1) * P)
                            for k in range(KT):
                                mm = split_mm(pe, out[:, tok], xt_hi[:, k, tok], xt_lo[:, k, tok],
                                              w_hi[:, k, cols], w_lo[:, k, cols], k == 0, k == KT - 1)
                    mm.then_inc(proj_done, 1)


def fourier(nc, name, tok0, seq_len, proj_d, w_fourier, chan_d, table_d, heads_d):
    NE, NO, W, CH = slices(seq_len)
    half = seq_len // 2
    EW, OW = NE * P, NO * P
    quads = [("e", a, min(a + 4, NE)) for a in range(0, NE, 4)] + [("o", a, min(a + 4, NO)) for a in range(0, NO, 4)]
    NQ = len(quads)
    with ExitStack() as outer:
        alo = Phase(nc, outer, name)
        z_hi = alo.sb("z_hi", [P, NE + NO, FOUR], F32R)
        z_lo = alo.sb("z_lo", [P, NE + NO, FOUR], F32R)
        bank = alo.ps("bank", [P, 8, 512])

        with ExitStack() as ctx:
            al = Phase(nc, ctx, name + "z")
            chan = al.sb("chan", [P, 2, P])
            wf = al.sb("wf", [P, NFG, P])
            ab_hi = al.sb("ab_hi", [P, 2, FOUR], F32R)
            ab_lo = al.sb("ab_lo", [P, 2, FOUR], F32R)
            u_raw = al.sb("u_raw", [P, 2, seq_len])
            fold = al.sb("fold", [P, EW + OW])
            f_hi = al.sb("f_hi", [P, 2, EW + OW], F32R)
            f_lo = al.sb("f_lo", [P, 2, EW + OW], F32R)

            in_ld, u_ld = al.sem("in_ld"), al.sems("u_ld", 2)
            ab_done, ab_hi_done, ab_split = al.sem("ab_done"), al.sem("ab_hi_done"), al.sem("ab_split")
            even_done, odd_done = al.sem("even_done"), al.sem("odd_done")
            f_hi_done, f_split = al.sem("f_hi_done"), al.sem("f_split")
            z_done, z_hi_done, z_split = al.sem("z_done"), al.sem("z_hi_done"), al.sem("z_split")
            block = ctx.enter_context(nc.Block())

            @block.sync
            def _(sp):
                sp.dma_start(chan[:], chan_d).then_inc(in_ld, 16)
                sp.dma_start(wf[:], w_fourier.rearrange("g c d -> c g d")).then_inc(in_ld, 16)
                for g in range(NFG):
                    if g >= 2:
                        sp.wait_ge(even_done, g - 1)
                        sp.wait_ge(odd_done, g - 1)
                    sp.dma_start(u_raw[:, g % 2, :], proj_d[g * P:(g + 1) * P, tok0:tok0 + seq_len]
                                 ).then_inc(u_ld[g % 2], 16)

            @block.gpsimd
            def _(pool):
                for g in range(NFG):
                    u = u_raw[:, g % 2, :]
                    pool.wait_ge(u_ld[g % 2], 16 * (g // 2 + 1))
                    if g:
                        pool.wait_ge(f_split, g)
                    pool.tensor_tensor(fold[:, EW:EW + 1], u[:, 0:1], u[:, 0:1], ALU.subtract)
                    pool.tensor_tensor(fold[:, EW + 1:EW + OW], u[:, 1:half],
                                       u[:, seq_len - 1:half:-1], ALU.subtract).then_inc(odd_done, 1)

            @block.vector
            def _(dve):
                for i in range(2):
                    dve.wait_ge(ab_hi_done, i + 1)
                    dve.tensor_tensor(ab_lo[:, i, :], bank[:, i, :], ab_hi[:, i, :].bitcast(F32),
                                      ALU.subtract).then_inc(ab_split, 1)

                def z_rest(g):
                    for q, (kind, a, b) in enumerate(quads):
                        base = a if kind == "e" else NE + a
                        out = slice(base, base + b - a)
                        cols = slice(g * P, (g + 1) * P)
                        dve.wait_ge(z_hi_done, g * NQ + q + 1)
                        dve.tensor_tensor(z_lo[:, out, cols],
                                          bank[:, 2 + q, 0:(b - a) * P].rearrange("p (s d) -> p s d", d=P),
                                          z_hi[:, out, cols].bitcast(F32), ALU.subtract).then_inc(z_split, 1)

                dve.memset(fold[:, half + 1:EW], 0.0)
                for g in range(NFG):
                    u = u_raw[:, g % 2, :]
                    dve.wait_ge(u_ld[g % 2], 16 * (g // 2 + 1))
                    if g:
                        dve.wait_ge(f_split, g)
                    dve.tensor_copy(fold[:, 0:1], u[:, 0:1])
                    dve.tensor_copy(fold[:, half:half + 1], u[:, half:half + 1])
                    dve.tensor_tensor(fold[:, 1:half], u[:, 1:half], u[:, seq_len - 1:half:-1], ALU.add)
                    dve.drain().then_inc(even_done, 1)
                    dve.wait_ge(f_hi_done, g + 1)
                    dve.tensor_tensor(f_lo[:, g % 2, :], fold[:], f_hi[:, g % 2, :].bitcast(F32), ALU.subtract
                                      ).then_inc(f_split, 1)
                    if g:
                        z_rest(g - 1)
                z_rest(NFG - 1)

            @block.scalar
            def _(act):
                for i in range(2):
                    act.wait_ge(ab_done, i + 1)
                    act.copy(ab_hi[:, i, :], bank[:, i, :]).then_inc(ab_hi_done, 1)

                def z_high(g):
                    for q, (kind, a, b) in enumerate(quads):
                        base = a if kind == "e" else NE + a
                        act.wait_ge(z_done, g * NQ + q + 1)
                        act.copy(z_hi[:, base:base + b - a, g * P:(g + 1) * P],
                                 bank[:, 2 + q, 0:(b - a) * P].rearrange("p (s d) -> p s d", d=P)
                                 ).then_inc(z_hi_done, 1)
                for g in range(NFG):
                    act.wait_ge(even_done, g + 1)
                    act.wait_ge(odd_done, g + 1)
                    if g >= 2:
                        act.wait_ge(z_done, NQ * (g - 1))
                    act.copy(f_hi[:, g % 2, :], fold[:]).then_inc(f_hi_done, 1)
                    if g:
                        z_high(g - 1)
                z_high(NFG - 1)

            @block.tensor
            def _(pe):
                pe.wait_ge(in_ld, 32)
                for i in range(2):
                    pe.matmul(bank[:, i, :], chan[:, i, :], wf[:].rearrange("p g d -> p (g d)"), start=True,
                              stop=True).then_inc(ab_done, 1)
                for g in range(NFG):
                    for q, (kind, a, b) in enumerate(quads):
                        if q == 0:
                            pe.wait_ge(f_split, g + 1)
                        if g == 0:
                            pe.wait_ge(ab_split, 2)
                        else:
                            pe.wait_ge(z_split, (g - 1) * NQ + q + 1)
                        i = int(kind == "o")
                        cols = slice(g * P, (g + 1) * P)
                        for s in range(a, b):
                            pos = slice((EW if i else 0) + s * P, (EW if i else 0) + (s + 1) * P)
                            mm = split_mm(pe, bank[:, 2 + q, (s - a) * P:(s - a + 1) * P],
                                          f_hi[:, g % 2, pos], f_lo[:, g % 2, pos], ab_hi[:, i, cols],
                                          ab_lo[:, i, cols], True, True)
                        mm.then_inc(z_done, 1)

        with ExitStack() as ctx:
            al = Phase(nc, ctx, name + "s")
            NT_ = NE + NO
            t_raw = al.sb("t_raw", [P, 4, W])
            slots = min(2, CH)
            t_hi = al.sb("t_hi", [P, slots, NT_, W], F32R)
            t_lo = al.sb("t_lo", [P, slots, NT_, W], F32R)
            odd = al.sb("odd", [P, 2, W])
            fwd = al.sb("fwd", [P, 2, W])
            rev = al.sb("rev", [P, 2, W])

            t_ld, t_hi_done, t_split = al.sems("t_ld", 4), al.sem("t_hi_done"), al.sem("t_split")
            even_done, odd_done, odd_read = al.sem("even_done"), al.sem("odd_done"), al.sem("odd_read")
            out_done, fwd_st, rev_st = al.sem("out_done"), al.sems("fwd_st", 2), al.sems("rev_st", 2)
            block = ctx.enter_context(nc.Block())

            @block.gpsimd
            def _(pool):
                for i in range(CH * NT_):
                    c, s = divmod(i, NT_)
                    if i >= 4:
                        pool.wait_ge(t_split, i - 3)
                    pool.dma_start(t_raw[:, i % 4, :], table_d[s * P:(s + 1) * P, c * W:(c + 1) * W]
                                   ).then_inc(t_ld[i % 4], 16)

            @block.scalar
            def _(act):
                def table(i):
                    c, s = divmod(i, NT_)
                    act.wait_ge(t_ld[i % 4], 16 * (i // 4 + 1))
                    if c >= slots:
                        act.wait_ge(even_done, NFG * (c - slots + 1))
                    act.copy(t_hi[:, c % slots, s, :], t_raw[:, i % 4, :]).then_inc(t_hi_done, 1)

                def copy_odd(n):
                    act.wait_ge(even_done, n + 1)
                    if n >= 2:
                        act.wait_ge(out_done, n - 1)
                    act.copy(odd[:, n % 2, :], bank[:, 2 * (n % 4) + 1, 0:W]).then_inc(odd_done, 1)
                ahead = list(range(CH * NT_))
                for i in range(min(slots * NT_, len(ahead))):
                    table(i)
                done = slots * NT_
                for n in range(CH * NFG):
                    copy_odd(n)
                    if n % NFG == NFG - 1:
                        while done < min((n // NFG + 1 + slots) * NT_, CH * NT_):
                            table(done)
                            done += 1

            @block.vector
            def _(dve):
                def rest(i):
                    c, s = divmod(i, NT_)
                    dve.wait_ge(t_hi_done, i + 1)
                    dve.tensor_tensor(t_lo[:, c % slots, s, :], t_raw[:, i % 4, :],
                                      t_hi[:, c % slots, s, :].bitcast(F32), ALU.subtract).then_inc(t_split, 1)

                def combine(n):
                    even = bank[:, 2 * (n % 4), 0:W]
                    dve.wait_ge(odd_done, n + 1)
                    if n >= 2:
                        dve.wait_ge(fwd_st[n % 2], 16 * (n // 2))
                        dve.wait_ge(rev_st[n % 2], 16 * (n // 2))
                    dve.tensor_tensor(fwd[:, n % 2, :], even, odd[:, n % 2, :], ALU.subtract)
                    dve.tensor_tensor(rev[:, n % 2, W - 1::-1], even, odd[:, n % 2, :], ALU.add)
                    dve.drain().then_inc(out_done, 1)
                done = min(slots, CH) * NT_
                for i in range(done):
                    rest(i)
                for n in range(CH * NFG):
                    combine(n)
                    if n % NFG == NFG - 1:
                        while done < min((n // NFG + 1 + slots) * NT_, CH * NT_):
                            rest(done)
                            done += 1

            @block.tensor
            def _(pe):
                for n in range(CH * NFG):
                    c, g = divmod(n, NFG)
                    cols = slice(g * P, (g + 1) * P)
                    if n >= 4:
                        pe.wait_ge(out_done, n - 3)
                    for s in range(NT_):
                        if g == 0:
                            pe.wait_ge(t_split, c * NT_ + s + 1)
                        which = int(s >= NE)
                        mm = split_mm(pe, bank[:, 2 * (n % 4) + which, 0:W], z_hi[:, s, cols], z_lo[:, s, cols],
                                      t_hi[:, c % slots, s, :], t_lo[:, c % slots, s, :], s in (0, NE),
                                      s in (NE - 1, NT_ - 1))
                    mm.then_inc(even_done, 1)

            @block.sync
            def _(sp):
                for n in range(CH * NFG):
                    c, g = divmod(n, NFG)
                    rows = slice(g * P, (g + 1) * P)
                    sp.wait_ge(out_done, n + 1)
                    sp.dma_start(heads_d[rows, tok0 + c * W:tok0 + (c + 1) * W], fwd[:, n % 2, :]
                                 ).then_inc(fwd_st[n % 2], 16)
                    sp.wait_ge(fwd_st[n % 2], 16 * (n // 2 + 1))
                    top = tok0 + seq_len - c * W + 1
                    sp.dma_start(heads_d[rows, top - W:top], rev[:, n % 2, :]).then_inc(rev_st[n % 2], 16)
                for s in range(2):
                    sp.wait_ge(rev_st[s], 16 * (CH * NFG // 2))


def attend(nc, proj_d, v_d, sink, bias_d, ident_d, heads_d):
    AHEAD = {"scores": 6, "bias": 5, "exp": 4, "turn": 3, "high": 2, "rest": 1, "values": 0}
    NB = NT
    PT_BANK = (0, 1, 2, 0, 1, 2, 0, 1)
    PT_BACK = (2, 2, 5, 3, 3, 3, 3, 3)
    with ExitStack() as ctx:
        al = Phase(nc, ctx, "c")
        ident = al.sb("ident", [P, P])
        bias = al.sb("bias", [P, NH, 3 * P])
        neg_sink = al.sb("neg_sink", [P, NH])
        snk = al.sb("snk", [P, NH])
        k_raw = al.sb("k_raw", [P, NKV, GRP])
        ka = al.sb("ka", [P, NKV, TOK], F32R)
        kb = al.sb("kb", [P, NKV, TOK], F32R)
        v_raw = al.sb("v_raw", [P, NB, NKV, HD])
        vv = al.sb("vv", [P, NB, NKV, 2, HD], F32R)
        q_raw = al.sb("q_raw", [P, 2, NH, P])
        qs = al.sb("qs", [P, 2, NH, P], F32R)
        prob = al.sb("prob", [P, 4, 3 * P])
        nmax = al.sb("nmax", [P, 2, NH])
        esink = al.sb("esink", [P, 2, NH])
        esum = al.sb("esum", [P, 2, NH])
        den = al.sb("den", [P, 2, NH])
        rden = al.sb("rden", [P, 2, NH])
        pt_hi = al.sb("pt_hi", [P, 4, 3 * P], F32R)
        pt_lo = al.sb("pt_lo", [P, 4, 3 * P], F32R)
        o_lo = al.sb("o_lo", [P, 2, NH, HD])
        o_sum = al.sb("o_sum", [P, 2, NH, HD])
        o_nrm = al.sb("o_nrm", [P, 2, NH, HD])
        ot = al.sb("ot", [P, 2, 4, P])
        sc = al.ps("sc", [P, 2, 512])
        pt = al.ps("pt", [P, 3, 512])
        tr = al.ps("tr", [P, 4, P])
        pv = al.ps("pv", [P, 2, 4, P])

        const_in, sink_neg = al.sem("const_in"), al.sem("sink_neg")
        k_ld, k_rounded, k_split = al.sem("k_ld"), al.sem("k_rounded"), al.sem("k_split")
        v_ld, v_hi_done, v_split = al.sem("v_ld"), al.sem("v_hi_done"), al.sem("v_split")
        q_ld, q_rounded, q_split = al.sems("q_ld", 2), al.sem("q_rounded"), al.sem("q_split")
        sc_done, biased, exp_done = al.sem("sc_done"), al.sem("biased"), al.sem("exp_done")
        pt_done, pt_hi_done, pt_split = al.sem("pt_done"), al.sem("pt_hi_done"), al.sem("pt_split")
        pv_done, sink_arg, sink_exp = al.sem("pv_done"), al.sem("sink_arg"), al.sem("sink_exp")
        o_lo_done, o_sum_done, o_nrm_done = al.sem("o_lo_done"), al.sem("o_sum_done"), al.sem("o_nrm_done")
        tr_done, ot_done, ot_st = al.sem("tr_done"), al.sem("ot_done"), al.sems("ot_st", 2)
        block = ctx.enter_context(nc.Block())

        FIRST, MID, LAST = (1, 2), (0, 1, 2), (0, 1)
        firsts = [t // P for t, _ in SEQS]
        lasts = [(t + s) // P - 1 for t, s in SEQS]

        def window(b):
            return FIRST if b in firsts else LAST if b in lasts else MID

        def blocks(eng, body):
            b = 0
            while b < NB:
                run = 0
                while b and b + run + 1 < NB and window(b + run) == MID and window(b + run + 1) == MID:
                    run += 1
                if run >= 4:
                    pairs = run // 2
                    with eng.Fori(0, pairs) as i:
                        for j in range(2):
                            body(i * 2 + (b + j), (b + j) % 2, MID, MID)
                    b += 2 * pairs
                else:
                    body(b, b % 2, window(b), window(b + 1) if b + 1 < NB else None)
                    b += 1

        def wait(eng, sem, count):
            if not isinstance(count, int) or count > 0:
                eng.wait_ge(sem, count)

        def at(stage, b, s, h, kbs, nxt):
            h += AHEAD[stage]
            if h >= NH:
                return (b + 1, 1 - s, h - NH, nxt) if nxt else None
            return (b, s, h, kbs) if h >= 0 else None

        def steps(eng, step, before):
            for h in range(-AHEAD["scores"], 0):
                step(0, 0, h, window(0), window(1))

            def body(b, s, kbs, nxt):
                for h in range(NH):
                    before(b, s, h, nxt)
                    step(b, s, h, kbs, nxt)
            blocks(eng, body)

        passed, passed_pool, passed_dve = al.sem("passed"), al.sem("passed_pool"), al.sem("passed_dve")
        heads_v = heads_d[FOUR:, :].rearrange("(k p) t -> p k t", p=P)
        q_view = proj_d[FOUR:KROW, :].rearrange("(h d) t -> d h t", d=HD)

        @block.sync
        def _(sp):
            sp.dma_start(bias[:], bias_d).then_inc(const_in, 16)
            sp.dma_start(snk[:], sink.partition_broadcast(P)).then_inc(const_in, 16)
            sp.dma_start(ident[:], ident_d).then_inc(const_in, 16)
            for g in range(NG):
                if g:
                    sp.wait_ge(k_split, 2 * g)
                for half in range(2):
                    sp.dma_start(k_raw[half * HD:(half + 1) * HD, :, :],
                                 proj_d[KROW:KROW + P, g * GRP:(g + 1) * GRP].rearrange("(v d) t -> d v t", d=HD)
                                 ).then_inc(k_ld, 16)
                if g == 0:
                    sp.dma_start(v_raw[:], v_d.rearrange("(b p) (v d) -> p b v d", p=P, d=HD)).then_inc(v_ld, 16)

            def store(b, s, kbs, nxt):
                sp.wait_ge(ot_done, b + 1)
                sp.sem_inc(passed, 1)
                sp.dma_start(heads_v[:, :, bass.ds(b * P, P)], ot[:, s, :, :]).then_inc(ot_st[s], 16)
            blocks(sp, store)
            for s in range(2):
                sp.wait_ge(ot_st[s], 16 * (NB // 2))

        @block.gpsimd
        def _(pool):
            def load_q(b, s):
                wait(pool, q_split, b - 1)
                for half in range(2):
                    pool.dma_start(q_raw[half * HD:(half + 1) * HD, s, :, :], q_view[:, :, bass.ds(b * P, P)]
                                   ).then_inc(q_ld[s], 16)

            def round_q(b, s):
                wait(pool, sc_done, (b - 1) * NH)
                pool.sem_inc(passed_pool, 1)
                pool.wait_ge(q_ld[s], (b - s) * 16 + 32)
                pool.sem_inc(passed_pool, 1)
                pool.tensor_copy(qs[:, s, :, :], q_raw[:, s, :, :]).then_inc(q_rounded, 1)

            def normalise(b, s):
                wait(pool, o_sum_done, b * 2 + 2)
                wait(pool, tr_done, b - 1)
                pool.tensor_tensor(o_nrm[:, s, :, :], o_sum[:, s, :, :],
                                   rden[:, s, :].unsqueeze(2).to_broadcast([P, NH, HD]), ALU.mult
                                   ).then_inc(o_nrm_done, 1)
            load_q(0, 0)
            load_q(1, 1)
            round_q(0, 0)
            round_q(1, 1)

            def body(b, s, kbs, nxt):
                if not isinstance(b, int) or b + 2 < NB:
                    load_q(b + 2, s)
                if not isinstance(b, int) or b > 0:
                    normalise(b - 1, 1 - s)
                if not isinstance(b, int) or b + 2 < NB:
                    round_q(b + 2, s)
            blocks(pool, body)
            normalise(NB - 1, (NB - 1) % 2)

        @block.vector
        def _(dve):
            dve.wait_ge(const_in, 48)
            dve.tensor_scalar(neg_sink[:], snk[:], -1.0, None, ALU.mult)
            for g in range(NG):
                tok = slice(g * GRP, (g + 1) * GRP)
                dve.wait_ge(k_rounded, 2 * g + 2)
                dve.tensor_tensor(kb[0:HD, :, tok], k_raw[0:HD, :, :], kb[0:HD, :, tok].bitcast(F32),
                                  ALU.subtract).then_inc(k_split, 1)
                dve.tensor_tensor(ka[HD:P, :, tok], k_raw[HD:P, :, :], ka[HD:P, :, tok].bitcast(F32),
                                  ALU.subtract).then_inc(k_split, 1)
            dve.wait_ge(v_hi_done, 1)
            dve.tensor_tensor(vv[:, :, :, 1, :], v_raw[:], vv[:, :, :, 0, :].bitcast(F32), ALU.subtract
                              ).then_inc(v_split, 1)

            def rest_q(b, s):
                dve.wait_ge(q_rounded, b + 1)
                dve.tensor_tensor(qs[HD:P, s, :, :], q_raw[HD:P, s, :, :], qs[HD:P, s, :, :].bitcast(F32),
                                  ALU.subtract).then_inc(q_split, 1)

            def add_bias(b, s, h, kbs):
                w = len(kbs) * P
                wait(dve, pt_done, b * NH + h - 3)
                dve.wait_ge(sc_done, b * NH + h + 1)
                dve.sem_inc(passed_dve, 1)
                dve.tensor_tensor_reduce(prob[:, h % 4, 0:w], sc[:, h % 2, 0:w],
                                         bias[:, h, kbs[0] * P:kbs[0] * P + w], 1.0, neg_sink[:, h:h + 1],
                                         ALU.add, ALU.min, nmax[:, s, h:h + 1]).then_inc(biased, 1)

            def rest_p(b, s, h, kbs):
                w = len(kbs) * P
                dve.wait_ge(pt_hi_done, b * NH + h + 1)
                dve.tensor_tensor(pt_lo[:, h % 4, 0:w], pt[:, PT_BANK[h], 0:w], pt_hi[:, h % 4, 0:w].bitcast(F32),
                                  ALU.subtract).then_inc(pt_split, 1)

            def denominators(b, s):
                dve.wait_ge(sink_exp, b + 1)
                dve.tensor_tensor(den[:, s, :], esum[:, s, :], esink[:, s, :], ALU.add)
                dve.drain()
                dve.reciprocal(rden[:, s, :], den[:, s, :])

            def sum_half(b, s, half):
                hs = slice(half * 4, half * 4 + 4)
                wait(dve, o_nrm_done, b - 1)
                dve.wait_ge(o_lo_done, b * 2 + (half + 1))
                dve.tensor_tensor(o_sum[:, s, hs, :], pv[:, half, :, 0:HD], o_lo[:, s, hs, :], ALU.add
                                  ).then_inc(o_sum_done, 1)

            def sink_minus_max(b, s):
                dve.drain()
                dve.tensor_tensor(esink[:, s, :], nmax[:, s, :], neg_sink[:], ALU.subtract
                                  ).then_inc(sink_arg, 1)

            def step(b, s, h, kbs, nxt):
                for stage, work in (("bias", add_bias), ("rest", rest_p)):
                    if (now := at(stage, b, s, h, kbs, nxt)):
                        work(*now)

            def before(b, s, h, nxt):
                later = not (isinstance(b, int) and b == 0)
                if h == 0 and nxt:
                    rest_q(b + 1, 1 - s)
                if h == 1 and later:
                    sum_half(b - 1, 1 - s, 1)
                if h == 3:
                    sink_minus_max(b, s)
                if h == 5:
                    sum_half(b, s, 0)
                    denominators(b, s)

            dve.drain()
            rest_q(0, 0)
            steps(dve, step, before)
            sum_half(NB - 1, (NB - 1) % 2, 1)

        @block.scalar
        def _(act):
            for g in range(NG):
                tok = slice(g * GRP, (g + 1) * GRP)
                act.wait_ge(k_ld, 32 * g + 32)
                act.copy(ka[:, :, tok], k_raw[:]).then_inc(k_rounded, 1)
                act.copy(kb[:, :, tok], k_raw[:]).then_inc(k_rounded, 1)
            act.wait_ge(v_ld, 16)
            act.copy(vv[:, :, :, 0, :], v_raw[:]).then_inc(v_hi_done, 1)

            def exponentials(b, s, h, kbs):
                w = len(kbs) * P
                act.wait_ge(biased, b * NH + h + 1)
                act.activation(prob[:, h % 4, 0:w], prob[:, h % 4, 0:w], ACT.Exp, bias=nmax[:, s, h:h + 1],
                               scale=-1.0, accum_out=esum[:, s, h:h + 1]).then_inc(exp_done, 1)

            def high_p(b, s, h, kbs):
                w = len(kbs) * P
                wait(act, pv_done, b * NH + h - 3)
                act.wait_ge(pt_done, b * NH + h + 1)
                act.copy(pt_hi[:, h % 4, 0:w], pt[:, PT_BANK[h], 0:w]).then_inc(pt_hi_done, 1)

            def low_half(b, s, half):
                hs = slice(half * 4, half * 4 + 4)
                wait(act, o_sum_done, b * 2 - 2)
                act.wait_ge(pv_done, b * NH + (half * 4 + 4))
                act.copy(o_lo[:, s, hs, :], pv[:, half, :, HD:P]).then_inc(o_lo_done, 1)

            def sinks(b, s):
                act.wait_ge(sink_arg, b + 1)
                act.activation(esink[:, s, :], esink[:, s, :], ACT.Exp).then_inc(sink_exp, 1)

            def outputs(b, s):
                act.wait_ge(tr_done, b + 1)
                wait(act, ot_st[s], (b - s) * 8)
                act.copy(ot[:, s, :, :], tr[:]).then_inc(ot_done, 1)

            def step(b, s, h, kbs, nxt):
                for stage, work in (("exp", exponentials), ("high", high_p)):
                    if (now := at(stage, b, s, h, kbs, nxt)):
                        work(*now)

            def before(b, s, h, nxt):
                later = not (isinstance(b, int) and b == 0)
                if h == 0 and later:
                    low_half(b - 1, 1 - s, 1)
                if h == 4:
                    sinks(b, s)
                    low_half(b, s, 0)
                if h == 6 and later:
                    outputs(b - 1, 1 - s)
            steps(act, step, before)
            low_half(NB - 1, (NB - 1) % 2, 1)
            outputs(NB - 1, (NB - 1) % 2)

        @block.tensor
        def _(pe):
            def scores(b, s, h, kbs):
                w = len(kbs) * P
                wait(pe, biased, b * NH + h - 1)
                if h == 0:
                    pe.wait_ge(q_split, b + 1)
                out, keys = sc[:, h % 2, 0:w], bass.ds((b + (kbs[0] - 1)) * P, w)
                pe.matmul(out, qs[:, s, h, :], kb[:, h // QPK, keys], start=True, stop=False)
                pe.matmul(out, qs[:, s, h, :], ka[:, h // QPK, keys], start=False, stop=True
                          ).then_inc(sc_done, 1)

            def turn(b, s, h, kbs):
                wait(pe, pt_split, b * NH + (h - PT_BACK[h] + 1))
                pe.wait_ge(exp_done, b * NH + h + 1)
                for i in range(len(kbs)):
                    mm = pe.transpose(pt[:, PT_BANK[h], i * P:(i + 1) * P], prob[:, h % 4, i * P:(i + 1) * P],
                                      ident[:])
                mm.then_inc(pt_done, 1)

            def values(b, s, h, kbs):
                if h % 4 == 0:
                    wait(pe, o_sum_done, b * 2 + (h // 4 - 1))
                pe.wait_ge(pt_split, b * NH + h + 1)
                for i, kb_ in enumerate(kbs):
                    keys = vv[:, bass.ds(b + (kb_ - 1), 1), h // QPK, :, :]
                    for half, p in enumerate((pt_lo, pt_hi)):
                        mm = pe.matmul(pv[:, h // 4, h % 4, :], p[:, h % 4, i * P:(i + 1) * P], keys,
                                       start=i + half == 0, stop=i == len(kbs) - 1 and half == 1)
                mm.then_inc(pv_done, 1)

            def outputs(b, s):
                wait(pe, ot_done, b)
                pe.wait_ge(o_nrm_done, b + 1)
                flat = o_nrm[:, s, :, :].rearrange("p h d -> p (h d)")
                for i in range(4):
                    mm = pe.transpose(tr[:, i, :], flat[:, i * P:(i + 1) * P], ident[:])
                mm.then_inc(tr_done, 1)

            pe.wait_ge(const_in, 48)
            pe.wait_ge(k_split, 2 * NG)
            pe.wait_ge(v_split, 1)

            def step(b, s, h, kbs, nxt):
                for stage, work in (("scores", scores), ("turn", turn), ("values", values)):
                    if (now := at(stage, b, s, h, kbs, nxt)):
                        work(*now)

            def before(b, s, h, nxt):
                if h == 5 and not (isinstance(b, int) and b == 0):
                    outputs(b - 1, 1 - s)
            steps(pe, step, before)
            outputs(NB - 1, (NB - 1) % 2)


def shape_constants():
    out = {"ident": np.eye(P, dtype=np.float32)}
    arg = 2 * np.pi * (np.outer(np.arange(P), np.arange(P)) % P) / P
    out["chan"] = np.stack([np.cos(arg), np.sin(arg)], axis=1).astype(np.float64) / math.sqrt(P)
    for i, (_, n) in enumerate(SEQS):
        ne, no, w, ch = slices(n)
        s, t = np.arange(ne * P)[:, None], np.arange(ch * w)[None, :]
        arg = 2 * np.pi * (s * t % n) / n
        out[f"table{i}"] = np.concatenate([np.cos(arg) * (s <= n // 2), np.sin(arg)[:no * P]], 0) / math.sqrt(n)
    rel = np.arange(3 * P)[None, :] - P - np.arange(P)[:, None]
    slope = 2.0 ** (-8.0 * (np.arange(NH) + 1) / NH)
    dist = np.abs(rel)
    out["bias"] = np.where(dist[:, None, :] <= P, slope[None, :, None] * dist[:, None, :], BIG)
    return {k: v.astype(np.float32) for k, v in out.items()}


def mix_out(nc, xn_d, heads_d, w_out, ln_g, ln_b, ident_d, x1_d, x1t_d):
    with ExitStack() as ctx:
        al = Phase(nc, ctx, "d")
        ident = al.sb("ident", [P, P])
        gain = al.sb("gain", [P, D])
        shift = al.sb("shift", [P, D])
        eps = al.sb("eps", [P, 1])
        mhalf = al.sb("mhalf", [P, 1])
        w_raw = al.sb("w_raw", [P, 2, D])
        w_hi = al.sb("w_hi", [P, KT, D], F32R)
        w_lo = al.sb("w_lo", [P, KT, D], F32R)
        h_raw = al.sb("h_raw", [P, 2, KT, P])
        h_hi = al.sb("h_hi", [P, 2, KT, P], F32R)
        h_lo = al.sb("h_lo", [P, 2, KT, P], F32R)
        xn = al.sb("xn", [P, 2, D])
        y = al.sb("y", [P, 2, D])
        yg = al.sb("yg", [P, 2, D])
        x1 = al.sb("x1", [P, 2, D])
        x1t = al.sb("x1t", [P, 2, KT, P])
        stats = al.sb("stats", [P, 2, 2, 6])
        mv = al.sb("mv", [P, 2, 2])
        var_eps = al.sb("var_eps", [P, 2])
        rstd = al.sb("rstd", [P, 2])
        mix = al.ps("mix", [P, 2, 2, 512])
        turn = al.ps("turn", [P, 2, 2, 512])

        const_in, const_set = al.sem("const_in"), al.sem("const_set")
        w_ld, w_hi_done, w_split = al.sems("w_ld", 2), al.sem("w_hi_done"), al.sem("w_split")
        h_ld, h_hi_done, h_split = al.sems("h_ld", 2), al.sem("h_hi_done"), al.sem("h_split")
        xn_ld, mix_done, y_done = al.sems("xn_ld", 2), al.sem("mix_done"), al.sem("y_done")
        stats_done, var_done, rstd_done = al.sem("stats_done"), al.sem("var_done"), al.sem("rstd_done")
        passed = al.sem("passed")
        x1_done, x1_st = al.sem("x1_done"), al.sems("x1_st", 2)
        turned, x1t_done, x1t_st = al.sem("turned"), al.sem("x1t_done"), al.sems("x1t_st", 2)

        heads_v = heads_d.rearrange("(k p) t -> p k t", p=P)
        x1t_v = x1t_d.rearrange("(k p) t -> p k t", p=P)
        block = ctx.enter_context(nc.Block())

        def tiles(eng, body):
            for s in range(2):
                body(s, s, True)
            with eng.Fori(1, NT // 2) as i:
                for s in range(2):
                    body(i * 2 + s, s, False)

        @block.sync
        def _(sp):
            sp.dma_start(gain[:], ln_g.partition_broadcast(P)).then_inc(const_in, 16)
            sp.dma_start(shift[:], ln_b.partition_broadcast(P)).then_inc(const_in, 16)
            sp.dma_start(ident[:], ident_d).then_inc(const_in, 16)
            for k in range(KT):
                if k >= 2:
                    sp.wait_ge(w_split, k - 1)
                sp.dma_start(w_raw[:, k % 2, :], w_out[k * P:(k + 1) * P, :]).then_inc(w_ld[k % 2], 16)

            def store(n, s, first):
                sp.wait_ge(x1_done, n + 1)
                sp.dma_start(x1_d[bass.ds(n * P, P), :], x1[:, s, :]).then_inc(x1_st[s], 16)
                sp.wait_ge(x1t_done, n + 1)
                sp.sem_inc(passed, 1)
                sp.dma_start(x1t_v[:, :, bass.ds(n * P, P)], x1t[:, s, :, :]).then_inc(x1t_st[s], 16)
            tiles(sp, store)
            for s in range(2):
                sp.wait_ge(x1_st[s], 16 * (NT // 2))
                sp.wait_ge(x1t_st[s], 16 * (NT // 2))

        @block.gpsimd
        def _(pool):
            def load(n, s, first):
                if not first:
                    pool.wait_ge(h_split, n - 1)
                pool.dma_start(h_raw[:, s, :, :], heads_v[:, :, bass.ds(n * P, P)]).then_inc(h_ld[s], 16)
                if not first:
                    pool.wait_ge(y_done, n - 1)
                pool.dma_start(xn[:, s, :], xn_d[bass.ds(n * P, P), :]).then_inc(xn_ld[s], 16)

            def inverse_std(n, s):
                pool.wait_ge(stats_done, n + 1)
                pool.tensor_tensor(var_eps[:, s:s + 1], mv[:, s, 1:2], eps[:], ALU.add).then_inc(var_done, 1)
                pool.wait_ge(var_done, n + 1)
                pool.tensor_tensor(rstd[:, s:s + 1], var_eps[:, s:s + 1], mhalf[:], ALU.pow
                                   ).then_inc(rstd_done, 1)
            load(0, 0, True)
            load(1, 1, True)
            pool.memset(eps[:], EPS).then_inc(const_set, 1)
            pool.memset(mhalf[:], -0.5).then_inc(const_set, 1)
            for k in range(KT):
                pool.wait_ge(w_hi_done, k + 1)
                pool.tensor_tensor(w_lo[:, k, :], w_raw[:, k % 2, :], w_hi[:, k, :].bitcast(F32),
                                   ALU.subtract).then_inc(w_split, 1)
            pool.wait_ge(const_set, 2)
            with pool.Fori(0, NT // 2 - 1) as i:
                for s in range(2):
                    inverse_std(i * 2 + s, s)
                    load(i * 2 + s + 2, s, False)
            for s in range(2):
                inverse_std(NT - 2 + s, s)

        @block.scalar
        def _(act):
            def split_heads(n, s, first):
                act.wait_ge(h_ld[s], (n - s) * 8 + 16)
                if not first:
                    act.wait_ge(mix_done, n - 1)
                act.copy(h_hi[:, s, :, :], h_raw[:, s, :, :]).then_inc(h_hi_done, 1)

            def evacuate_turned(n, s, first):
                act.wait_ge(turned, n + 1)
                if not first:
                    act.wait_ge(x1t_st[s], (n - s) * 8)
                act.copy(x1t[:, s, :, :].rearrange("p k c -> p (k c)"),
                         turn[:, s, :, :].rearrange("p a c -> p (a c)")).then_inc(x1t_done, 1)
            split_heads(0, 0, True)
            split_heads(1, 1, True)
            for k in range(KT):
                act.wait_ge(w_ld[k % 2], 16 * (k // 2 + 1))
                act.copy(w_hi[:, k, :], w_raw[:, k % 2, :]).then_inc(w_hi_done, 1)
            split_heads(2, 0, False)
            evacuate_turned(0, 0, True)
            split_heads(3, 1, False)
            evacuate_turned(1, 1, True)
            with act.Fori(1, NT // 2 - 1) as i:
                for s in range(2):
                    split_heads(i * 2 + s + 2, s, False)
                    evacuate_turned(i * 2 + s, s, False)
            for s in range(2):
                evacuate_turned(NT - 2 + s, s, False)

        @block.vector
        def _(dve):
            def rest_of_heads(n, s):
                dve.wait_ge(h_hi_done, n + 1)
                dve.tensor_tensor(h_lo[:, s, :, :], h_raw[:, s, :, :], h_hi[:, s, :, :].bitcast(F32),
                                  ALU.subtract).then_inc(h_split, 1)

            def norm(n, s, first):
                dve.wait_ge(mix_done, n + 1)
                dve.wait_ge(xn_ld[s], (n - s) * 8 + 16)
                for h in range(2):
                    cols = slice(h * 512, (h + 1) * 512)
                    add = dve.scalar_tensor_tensor(y[:, s, cols], xn[:, s, cols], ALPHA, mix[:, s, h, :],
                                                   ALU.mult, ALU.add)
                add.then_inc(y_done, 1)
                dve.drain()
                for h in range(2):
                    dve.bn_stats(stats[:, s, h, :], y[:, s, h * 512:(h + 1) * 512])
                dve.drain()
                dve.bn_aggr(mv[:, s, :], stats[:, s, :, :]).then_inc(stats_done, 1)
                dve.drain()
                if first and s == 0:
                    dve.wait_ge(const_in, 48)
                dve.scalar_tensor_tensor(yg[:, s, :], y[:, s, :], mv[:, s, 0:1], gain[:], ALU.subtract,
                                         ALU.mult)
                dve.drain()
                dve.wait_ge(rstd_done, n + 1)
                if not first:
                    dve.wait_ge(turned, n - 1)
                    dve.wait_ge(x1_st[s], (n - s) * 8)
                dve.scalar_tensor_tensor(x1[:, s, :], yg[:, s, :], rstd[:, s:s + 1], shift[:], ALU.mult,
                                         ALU.add).then_inc(x1_done, 1)
            rest_of_heads(0, 0)
            rest_of_heads(1, 1)
            for s in range(2):
                norm(s, s, True)
                rest_of_heads(s + 2, s)
            with dve.Fori(1, NT // 2 - 1) as i:
                for s in range(2):
                    norm(i * 2 + s, s, False)
                    rest_of_heads(i * 2 + s + 2, s)
            for s in range(2):
                norm(NT - 2 + s, s, False)

        @block.tensor
        def _(pe):
            def product(n, s, first):
                for h in range(2):
                    cols = slice(h * 512, (h + 1) * 512)
                    for k in range(KT):
                        if h == 0 and k == 0:
                            pe.wait_ge(h_split, n + 1)
                            if not first:
                                pe.wait_ge(y_done, n - 1)
                        if first and h == 0 and s == 0:
                            pe.wait_ge(w_split, k + 1)
                        mm = split_mm(pe, mix[:, s, h, :], h_hi[:, s, k, :], h_lo[:, s, k, :],
                                      w_hi[:, k, cols], w_lo[:, k, cols], k == 0, k == KT - 1)
                mm.then_inc(mix_done, 1)

            def transpose(n, s, first):
                for k in range(KT):
                    if k == 0:
                        pe.wait_ge(x1_done, n + 1)
                        if not first:
                            pe.wait_ge(x1t_done, n - 1)
                    mm = pe.transpose(turn[:, s, k // 4, (k % 4) * P:(k % 4 + 1) * P],
                                      x1[:, s, k * P:(k + 1) * P], ident[:])
                mm.then_inc(turned, 1)
            pe.wait_ge(const_in, 48)
            product(0, 0, True)
            product(1, 1, True)
            product(2, 0, False)
            transpose(0, 0, True)
            product(3, 1, False)
            transpose(1, 1, True)
            with pe.Fori(1, NT // 2 - 1) as i:
                for s in range(2):
                    product(i * 2 + s + 2, s, False)
                    transpose(i * 2 + s, s, False)
            for s in range(2):
                transpose(NT - 2 + s, s, False)


def mlp(nc, x1_d, x1t_d, w1_d, w2_d, ln_g, ln_b, out_d):
    UC = 4
    NC = FF // (UC * P)
    NO = 2 * TPG
    OPU = NO // UC
    BANKS = 4
    with ExitStack() as ctx:
        al = Phase(nc, ctx, "e")
        gain = al.sb("gain", [P, D])
        shift = al.sb("shift", [P, D])
        eps = al.sb("eps", [P, TPG])
        mhalf = al.sb("mhalf", [P, TPG])
        xt_raw = al.sb("xt_raw", [P, 2, GRP])
        xt_hi = al.sb("xt_hi", [P, KT, GRP], F32R)
        xt_lo = al.sb("xt_lo", [P, KT, GRP], F32R)
        w1_raw = al.sb("w1_raw", [P, 2, KT * P])
        w1_hi = al.sb("w1_hi", [P, 2, KT * P], F32R)
        w1_lo = al.sb("w1_lo", [P, 2, KT * P], F32R)
        w2_raw = al.sb("w2_raw", [P, 2, D])
        w2_hi = al.sb("w2_hi", [P, 2, UC, D], F32R)
        w2_lo = al.sb("w2_lo", [P, 2, UC, D], F32R)
        relu = al.sb("relu", [P, 4, GRP])
        hid = al.sb("hid", [P, 2, GRP])
        h_hi = al.sb("h_hi", [P, 2, UC, GRP], F32R)
        h_lo = al.sb("h_lo", [P, 2, UC, GRP], F32R)
        acc = al.sb("acc", [P, TPG, D])
        stats = al.sb("stats", [P, TPG, 2, 6])
        mv = al.sb("mv", [P, TPG, 2])
        var_eps = al.sb("var_eps", [P, TPG])
        rstd = al.sb("rstd", [P, TPG])
        up = al.ps("up", [P, BANKS, 512])
        down = al.ps("down", [P, BANKS, 512])

        const_in, const_set = al.sem("const_in"), al.sem("const_set")
        xt_ld, xt_hi_done = al.sems("xt_ld", 2), al.sem("xt_hi_done")
        xt_split = al.sem("xt_split")
        w1_ld, w1_hi_done = al.sems("w1_ld", 2), al.sem("w1_hi_done")
        w1_split = al.sem("w1_split")
        w2_ld, w2_hi_done = al.sems("w2_ld", 2), al.sem("w2_hi_done")
        w2_split = al.sem("w2_split")
        up_done = al.sem("up_done")
        relu_done = al.sem("relu_done")
        h_hi_done = al.sem("h_hi_done")
        h_split = al.sem("h_split")
        down_done = al.sem("down_done")
        down_read = al.sem("down_read")
        x1_ld = al.sems("x1_ld", TPG)
        stats_done, var_done, rstd_done = al.sem("stats_done"), al.sem("var_done"), al.sem("rstd_done")
        y_done, y_st = al.sem("y_done"), al.sems("y_st", TPG)
        DOWN0 = NO + 1

        block = ctx.enter_context(nc.Block())

        def chunks(eng, g, body):
            with eng.Fori(1, NC // 2) as i:
                for s in range(2):
                    body(g, i * 2 + s, s)

        @block.sync
        def _(sp):
            def store_y(g):
                for t in range(TPG):
                    sp.wait_ge(y_done, g * TPG + t + 1)
                    sp.dma_start(out_d[bass.ds(g * GRP + t * P, P), :], acc[:, t, :]).then_inc(y_st[t], 16)

            def load_w1(n, slot, tile):
                sp.wait_ge(w1_split, n + 1)
                sp.dma_start(w1_raw[:, slot, :], w1_d[bass.ds(tile * P, P), :]).then_inc(w1_ld[slot], 16)

            def load_w2(n, slot, tile):
                sp.wait_ge(w2_split, n + 1)
                sp.dma_start(w2_raw[:, slot, :], w2_d[bass.ds(tile * P, P), :]).then_inc(w2_ld[slot], 16)

            def load_chunk(g, c, units=range(UC), last=False):
                for u in units:
                    n = g * (NC * UC) + c * UC + u
                    load_w1(n + 2, u % 2, u + 2 - UC if last and u + 2 >= UC else c * UC + (u + 2))
                    load_w2(n, u % 2, c * UC + u)

            def group(g, first):
                for k in range(KT):
                    sp.wait_ge(xt_split, g * KT + k + 1)
                    sp.dma_start(xt_raw[:, k % 2, :], x1t_d[k * P:(k + 1) * P, bass.ds(g * GRP, GRP)]
                                 ).then_inc(xt_ld[k % 2], 16)
                load_chunk(g, 0)
                load_chunk(g, 1, range(1))
                if not first:
                    store_y(g - 1)
                for t in range(TPG):
                    if not first:
                        sp.wait_ge(y_st[t], g * 16)
                    sp.dma_start(acc[:, t, :], x1_d[bass.ds(g * GRP + t * P, P), :]).then_inc(x1_ld[t], 16)
                load_chunk(g, 1, range(1, UC))
                with sp.Fori(2, NC - 1) as c:
                    load_chunk(g, c)
                load_chunk(g, NC - 1, last=True)

            sp.dma_start(gain[:], ln_g.partition_broadcast(P)).then_inc(const_in, 16)
            sp.dma_start(shift[:], ln_b.partition_broadcast(P)).then_inc(const_in, 16)
            load_w1(0, 0, 0)
            load_w1(1, 1, 1)
            group(0, True)
            with sp.Fori(1, NG) as g:
                group(g, False)
            store_y(NG - 1)
            for t in range(TPG):
                sp.wait_ge(y_st[t], NG * 16)

        @block.gpsimd
        def _(pool):
            def x1_lows(g):
                for k in range(KT):
                    pool.wait_ge(xt_hi_done, g * KT + k + 1)
                    pool.tensor_tensor(xt_lo[:, k, :], xt_raw[:, k % 2, :], xt_hi[:, k, :].bitcast(F32),
                                       ALU.subtract).then_inc(xt_split, 1)

            def w1_low(n, slot):
                pool.wait_ge(w1_hi_done, n + 1)
                pool.tensor_tensor(w1_lo[:, slot, :], w1_raw[:, slot, :], w1_hi[:, slot, :].bitcast(F32),
                                   ALU.subtract).then_inc(w1_split, 1)

            def w1_lows(g):
                with pool.Fori(0, NC) as c:
                    for u in range(UC):
                        w1_low(g * (NC * UC) + c * UC + (u + 2), u % 2)

            def inverse_std(g):
                pool.wait_ge(stats_done, g * TPG + TPG)
                pool.tensor_tensor(var_eps[:], mv[:, :, 1], eps[:], ALU.add).then_inc(var_done, 1)
                pool.wait_ge(var_done, g + 1)
                pool.tensor_tensor(rstd[:], var_eps[:], mhalf[:], ALU.pow).then_inc(rstd_done, 1)

            pool.sem_inc(xt_split, 2)
            pool.sem_inc(w1_split, 2)
            pool.memset(eps[:], EPS).then_inc(const_set, 1)
            pool.memset(mhalf[:], -0.5).then_inc(const_set, 1)
            w1_low(0, 0)
            w1_low(1, 1)
            x1_lows(0)
            w1_lows(0)
            pool.wait_ge(const_set, 2)
            with pool.Fori(1, NG) as g:
                x1_lows(g)
                inverse_std(g - 1)
                w1_lows(g)
            inverse_std(NG - 1)

        @block.scalar
        def _(act):
            def w1_high(n, u):
                act.wait_ge(w1_ld[u % 2], (n - u % 2) * 8 + 16)
                act.wait_ge(up_done, n + 1)
                act.copy(w1_hi[:, u % 2, :], w1_raw[:, u % 2, :]).then_inc(w1_hi_done, 1)

            def chunk(g, c, s):
                for u in range(UC):
                    n = g * (NC * UC) + c * UC + u
                    w1_high(n + 2, u)
                    act.wait_ge(up_done, n + 3)
                    act.wait_ge(h_split, n + 1)
                    act.activation(relu[:, u % 4, :], up[:, u % BANKS, :], ACT.Relu).then_inc(relu_done, 1)
                    act.wait_ge(relu_done, n + 1 + BANKS)
                    act.wait_ge(down_done, g * (NC * NO) + c * NO + (DOWN0 - NO))
                    act.activation(h_hi[:, s, u, :], relu[:, u % 4, :], ACT.Square).then_inc(h_hi_done, 1)
                    act.wait_ge(w2_ld[u % 2], (n - u % 2) * 8 + 16)
                    act.copy(w2_hi[:, s, u, :], w2_raw[:, u % 2, :]).then_inc(w2_hi_done, 1)

            act.sem_inc(relu_done, BANKS)
            w1_high(0, 0)
            w1_high(1, 1)
            with act.Fori(0, NG) as g:
                for k in range(KT):
                    act.wait_ge(xt_ld[k % 2], g * (KT * 8) + (k // 2) * 16 + 16)
                    act.wait_ge(up_done, g * (NC * UC) + 2)
                    act.copy(xt_hi[:, k, :], xt_raw[:, k % 2, :]).then_inc(xt_hi_done, 1)
                with act.Fori(0, NC // 2) as i:
                    for s in range(2):
                        chunk(g, i * 2 + s, s)

        @block.vector
        def _(dve):
            def unit(g, c, s, u):
                n = g * (NC * UC) + c * UC + u
                dve.wait_ge(relu_done, n + 1 + BANKS)
                dve.tensor_tensor(hid[:, u % 2, :], relu[:, u % 4, :], relu[:, u % 4, :], ALU.mult)
                dve.drain()
                dve.wait_ge(h_hi_done, n + 1)
                dve.tensor_tensor(h_lo[:, s, u, :], hid[:, u % 2, :], h_hi[:, s, u, :].bitcast(F32),
                                  ALU.subtract).then_inc(h_split, 1)
                dve.wait_ge(w2_hi_done, n + 1)
                dve.tensor_tensor(w2_lo[:, s, u, :], w2_raw[:, u % 2, :], w2_hi[:, s, u, :].bitcast(F32),
                                  ALU.subtract).then_inc(w2_split, 1)

            def add(g, c, o):
                t, cols = o // 2, slice((o % 2) * 512, (o % 2 + 1) * 512)
                dve.wait_ge(down_done, g * (NC * NO) + c * NO + (o + 1 + DOWN0))
                dve.tensor_tensor(acc[:, t, cols], down[:, o % BANKS, :], acc[:, t, cols], ALU.add
                                  ).then_inc(down_read, 1)

            def chunk(g, c, s):
                for u in range(UC):
                    unit(g, c, s, u)
                    for o in range(u * OPU, (u + 1) * OPU):
                        add(g, c - 1, o)

            def norm(g):
                dve.drain()
                for t in range(TPG):
                    dve.bn_aggr(mv[:, t, :], stats[:, t, :, :]).then_inc(stats_done, 1)
                dve.drain()
                for t in range(TPG):
                    dve.scalar_tensor_tensor(acc[:, t, :], acc[:, t, :], mv[:, t, 0:1], gain[:],
                                             ALU.subtract, ALU.mult)
                dve.drain()
                for t in range(TPG):
                    dve.wait_ge(rstd_done, g + 1)
                    dve.scalar_tensor_tensor(acc[:, t, :], acc[:, t, :], rstd[:, t:t + 1], shift[:],
                                             ALU.mult, ALU.add).then_inc(y_done, 1)

            dve.sem_inc(h_split, 4)
            dve.sem_inc(w2_split, 2)
            dve.sem_inc(down_read, BANKS)
            dve.wait_ge(const_in, 32)
            with dve.Fori(0, NG) as g:
                for u in range(UC):
                    unit(g, 0, 0, u)
                for t in range(TPG):
                    dve.wait_ge(x1_ld[t], g * 16 + 16)
                    dve.tensor_scalar(acc[:, t, :], acc[:, t, :], ALPHA, None, ALU.mult)
                chunk(g, 1, 1)
                chunks(dve, g, chunk)
                for o in range(NO):
                    add(g, NC - 1, o)
                    if o % 2:
                        dve.drain()
                        for h in range(2):
                            dve.bn_stats(stats[:, o // 2, h, :], acc[:, o // 2, h * 512:(h + 1) * 512])
                norm(g)

        @block.tensor
        def _(pe):
            def unit(g, c, s, u):
                n = g * (NC * UC) + c * UC + u
                for k in range(KT):
                    if isinstance(c, int) and c == 0 and u == 0:
                        pe.wait_ge(xt_split, g * KT + k + 3)
                    if k == 0:
                        pe.wait_ge(w1_split, n + 3)
                        pe.wait_ge(relu_done, n + 1)
                    cols = slice(k * P, (k + 1) * P)
                    mm = split_mm(pe, up[:, u % BANKS, :], w1_hi[:, u % 2, cols], w1_lo[:, u % 2, cols],
                                  xt_hi[:, k, :], xt_lo[:, k, :], k == 0, k == KT - 1)
                mm.then_inc(up_done, 1)

            def output(g, c, s, o):
                tok, cols = slice((o // 2) * P, (o // 2 + 1) * P), slice((o % 2) * 512, (o % 2 + 1) * 512)
                for k in range(UC):
                    if o == 0:
                        n = g * (NC * UC) + c * UC + k
                        pe.wait_ge(h_split, n + 5)
                        pe.wait_ge(w2_split, n + 3)
                    if k == 0:
                        pe.wait_ge(down_read, g * (NC * NO) + c * NO + (o + 1))
                    mm = split_mm(pe, down[:, o % BANKS, :], h_hi[:, s, k, tok], h_lo[:, s, k, tok],
                                  w2_hi[:, s, k, cols], w2_lo[:, s, k, cols], k == 0, k == UC - 1)
                mm.then_inc(down_done, 1)

            def chunk(g, c, s):
                for u in range(UC):
                    unit(g, c, s, u)
                    for o in range(u * OPU, (u + 1) * OPU):
                        output(g, c - 1, 1 - s, o)

            pe.sem_inc(up_done, 2)
            pe.sem_inc(down_done, DOWN0)
            with pe.Fori(0, NG) as g:
                for u in range(UC):
                    unit(g, 0, 0, u)
                chunk(g, 1, 1)
                chunks(pe, g, chunk)
                for o in range(NO):
                    output(g, NC - 1, 1, o)



def build(nc, d, s, y):
    embed_project(nc, d["x"], d["ln_emb_g"], d["ln_emb_b"], d["w_in"], d["ident"], s["x_norm"], s["proj"],
                  s["v"])
    for i, (tok0, seq_len) in enumerate(SEQS):
        fourier(nc, f"b{i}", tok0, seq_len, s["proj"], d["w_fourier"], d["chan"], d[f"table{i}"], s["heads"])
    attend(nc, s["proj"], s["v"], d["sink"], d["bias"], d["ident"], s["heads"])
    mix_out(nc, s["x_norm"], s["heads"], d["w_out"], d["ln_mix_g"], d["ln_mix_b"], d["ident"], s["x1"], s["x1t"])
    mlp(nc, s["x1"], s["x1t"], d["w_ff1"], d["w_ff2"], d["ln_ffn_g"], d["ln_ffn_b"], y)


def kernel(x_prompt, x_sample, ln_emb_g, ln_emb_b, w_in, w_fourier, sink_logits, w_out, ln_mix_g, ln_mix_b,
           w_ff1, w_ff2, ln_ffn_g, ln_ffn_b):
    import concourse.bacc as bacc
    from concourse.bass_utils import run_bass_kernel_spmd
    nc = bacc.Bacc("TRN2", target_bir_lowering=False, num_devices=1)
    host = {
        "x": np.concatenate([np.asarray(x_prompt)[0], np.asarray(x_sample)[0]], axis=0),
        "ln_emb_g": ln_emb_g, "ln_emb_b": ln_emb_b,
        "w_in": np.asarray(w_in)[0], "w_fourier": np.asarray(w_fourier)[0], "sink": np.asarray(sink_logits)[0],
        "w_out": np.asarray(w_out)[0], "ln_mix_g": np.asarray(ln_mix_g)[0], "ln_mix_b": np.asarray(ln_mix_b)[0],
        "w_ff1": np.asarray(w_ff1)[0].reshape(KT, P, FF // P, P).transpose(2, 1, 0, 3).reshape(FF, D),
        "w_ff2": np.asarray(w_ff2)[0], "ln_ffn_g": np.asarray(ln_ffn_g)[0], "ln_ffn_b": np.asarray(ln_ffn_b)[0],
        **shape_constants(),
    }
    host = {k: np.ascontiguousarray(v) for k, v in host.items()}
    d = {k: nc.dram_tensor(k, v.shape, F32, kind="ExternalInput").ap() for k, v in host.items()}
    scratch = {"x_norm": (TOK, D), "proj": (FT * P, TOK), "v": (TOK, P), "heads": (D, TOK + 2),
               "x1": (TOK, D), "x1t": (D, TOK)}
    s = {k: nc.dram_tensor(f"s_{k}", shape, F32, kind="Internal").ap() for k, shape in scratch.items()}
    y = nc.dram_tensor("y", (TOK, D), F32, kind="ExternalOutput").ap()
    build(nc, d, s, y)
    got = run_bass_kernel_spmd(nc, [host], core_ids=[0]).results[0]["y"]
    return tuple(got[None, t:t + n] for t, n in SEQS)
```
